# Optimizing a Trainium2 kernel written in Bass

```python
import math
import jax
import jax.numpy as jnp
from jax import lax
import numpy as np

D_MODEL = 1024
BATCH = 1
SEQ = 128
DEPTH = 2
DEC_BATCH = 1
DEC_SEQ = 256
PAST_LEN = 128

GRID_W = 64
N_ATTN_LAYERS = (DEPTH + 1) // 2
N_HYENA_LAYERS = DEPTH // 2
MLA_HEADS = 8
Q_RANK = 384
KV_RANK = 128
NOPE_DIM = 64
ROPE_DIM = 32
V_DIM = 64
QK_DIM = NOPE_DIM + ROPE_DIM
ROPE_THETA = 10000.0
NA_HEADS = 8
NA_HEAD_DIM = 64
NA_KH = 8
NA_KW = 16
NA_KBW = 2 * NA_KW
NA_WIDTH = NA_HEADS * NA_HEAD_DIM
ATTN_IN = Q_RANK + KV_RANK + ROPE_DIM + 3 * NA_WIDTH
ATTN_OUT = MLA_HEADS * V_DIM + NA_WIDTH
Q_BLOCK = 128
HY_ORDER = 2
HY_BANDS = 8
HY_EMB = 1 + 2 * HY_BANDS
HY_FF = 64
HY_SHORT = 3
HY_TARGET = 1e-2
HY_FAST_DECAY = 0.3
HY_SLOW_DECAY = 1.5
HY_MOD_SHIFT = 0.05
N_GROUPS = 4
EXPERTS_PER_GROUP = 8
N_EXPERTS = N_GROUPS * EXPERTS_PER_GROUP
TOP_K = 2
D_EXPERT = 256
EPS = 1e-6
NEG_INF = -1e30

kernel_name = 'hybrid_mla_natten_hyena_hmoe_step'

def rmsnorm(x, g):
    x32 = x.astype(jnp.float32)
    y = x32 * lax.rsqrt(jnp.mean(x32 * x32, axis=-1, keepdims=True) + EPS)
    return (y * g.astype(jnp.float32)).astype(x.dtype)

def adaln(cvec, w, b):
    m = jax.nn.silu(cvec) @ w + b
    return [t[:, None, :] for t in jnp.split(m, 6, axis=-1)]

def blocked_attention(q, k, v, scale):
    B, Lq, H, dk = q.shape
    nblk = Lq // Q_BLOCK
    qb = jnp.moveaxis(q.reshape(B, nblk, Q_BLOCK, H, dk), 1, 0)

    def one_block(qblk):
        s = jnp.einsum('bqhd,bkhd->bhqk', qblk, k).astype(jnp.float32) * scale
        p = jax.nn.softmax(s, axis=-1).astype(v.dtype)
        return jnp.einsum('bhqk,bkhd->bqhd', p, v)

    o = lax.map(one_block, qb)
    return jnp.moveaxis(o, 0, 1).reshape(B, Lq, H, v.shape[-1])

def axial_rope(x):
    L = x.shape[1]
    t = jnp.arange(L)
    quarter = ROPE_DIM // 4
    inv = ROPE_THETA ** (-jnp.arange(quarter, dtype=jnp.float32) / quarter)

    def rot(xp, pos):
        ang = pos.astype(jnp.float32)[:, None] * inv[None, :]
        cos = jnp.cos(ang)[None, :, None, :]
        sin = jnp.sin(ang)[None, :, None, :]
        x1, x2 = jnp.split(xp.astype(jnp.float32), 2, axis=-1)
        return jnp.concatenate([x1 * cos - x2 * sin, x2 * cos + x1 * sin], axis=-1)

    x_nope, x_row, x_col = jnp.split(x, [NOPE_DIM, NOPE_DIM + ROPE_DIM // 2], axis=-1)
    out = jnp.concatenate([x_nope.astype(jnp.float32), rot(x_row, t // GRID_W), rot(x_col, t % GRID_W)], axis=-1)
    return out.astype(x.dtype)

def mla_expand(ckv, k_rope, w_kv_up, k_gain):
    B, L, _ = ckv.shape
    kv = (ckv @ w_kv_up).reshape(B, L, MLA_HEADS, NOPE_DIM + V_DIM)
    k_nope, v = jnp.split(kv, [NOPE_DIM], axis=-1)
    k_pe = jnp.broadcast_to(k_rope[:, :, None, :], (B, L, MLA_HEADS, ROPE_DIM))
    k = rmsnorm(jnp.concatenate([k_nope, k_pe], axis=-1), k_gain)
    return k, v

def attn_in_proj(h, w_in, q_norm, kv_norm, w_q_up, w_kv_up, q_gain, k_gain, na_q_gain, na_k_gain):
    B, L, _ = h.shape
    p = h @ w_in
    q_lat, kv_lat, k_rope, na_qkv = jnp.split(p, [Q_RANK, Q_RANK + KV_RANK, Q_RANK + KV_RANK + ROPE_DIM], axis=-1)
    q = rmsnorm((rmsnorm(q_lat, q_norm) @ w_q_up).reshape(B, L, MLA_HEADS, QK_DIM), q_gain)
    ckv = rmsnorm(kv_lat, kv_norm)
    k, v = mla_expand(ckv, k_rope, w_kv_up, k_gain)
    na_qkv = na_qkv.reshape(B, L, 3, NA_HEADS, NA_HEAD_DIM)
    nq = rmsnorm(na_qkv[:, :, 0], na_q_gain)
    nk = rmsnorm(na_qkv[:, :, 1], na_k_gain)
    nv = na_qkv[:, :, 2]
    return q, k, v, ckv, k_rope, nq, nk, nv

def na_layout(rows):
    wh = min(NA_KH, rows)
    ncb = GRID_W // NA_KW
    r = np.arange(rows)
    rs = np.clip(r - wh // 2, 0, rows - wh)
    key_rows = rs[:, None] + np.arange(wh)[None, :]
    kb = np.clip(np.arange(ncb) * NA_KW - NA_KW // 2, 0, GRID_W - NA_KBW)
    key_cols = kb[:, None] + np.arange(NA_KBW)[None, :]
    key_idx = key_rows[:, None, :, None] * GRID_W + key_cols[None, :, None, :]
    q_cols = np.arange(ncb)[:, None] * NA_KW + np.arange(NA_KW)[None, :]
    cs = np.clip(q_cols - NA_KW // 2, 0, GRID_W - NA_KW)
    col_ok = (key_cols[:, None, :] >= cs[:, :, None]) & (key_cols[:, None, :] < cs[:, :, None] + NA_KW)
    valid = np.broadcast_to(col_ok[:, :, None, :], (ncb, NA_KW, wh, NA_KBW)).reshape(ncb, NA_KW, wh * NA_KBW)
    dy = key_rows - r[:, None] + NA_KH - 1
    dx = np.clip(key_cols[:, None, :] - q_cols[:, :, None], -(NA_KW - 1), NA_KW - 1) + NA_KW - 1
    return key_idx.reshape(rows, ncb, wh * NA_KBW), valid, dy, dx, wh

def neighbourhood_attention(q, k, v, k_ctx, v_ctx, rpb):
    B, L, H, d = q.shape
    rows = L // GRID_W
    ncb = GRID_W // NA_KW
    key_idx, valid, dy, dx, wh = na_layout(rows)
    nk = wh * NA_KBW
    scale = d ** -0.5
    flat_idx = jnp.asarray(key_idx.reshape(-1))
    qb = q.reshape(B, rows, ncb, NA_KW, H, d)
    kg = jnp.take(k, flat_idx, axis=1).reshape(B, rows, ncb, nk, H, d)
    vg = jnp.take(v, flat_idx, axis=1).reshape(B, rows, ncb, nk, H, d)
    bias = rpb[:, dy[:, None, None, :, None], dx[None, :, :, None, :]].reshape(H, rows, ncb, NA_KW, nk)
    bias = jnp.transpose(bias, (1, 2, 0, 3, 4)).astype(jnp.float32)
    s_win = jnp.einsum('brjqhd,brjkhd->brjhqk', qb, kg).astype(jnp.float32) * scale + bias[None]
    s_win = jnp.where(jnp.asarray(valid)[None, None, :, None], s_win, NEG_INF)
    s_ctx = jnp.einsum('brjqhd,bchd->brjhqc', qb, k_ctx).astype(jnp.float32) * scale
    p = jax.nn.softmax(jnp.concatenate([s_win, s_ctx], axis=-1), axis=-1).astype(v.dtype)
    o = (jnp.einsum('brjhqk,brjkhd->brjqhd', p[..., :nk], vg)
         + jnp.einsum('brjhqc,bchd->brjqhd', p[..., nk:], v_ctx))
    return o.reshape(B, L, H, d)

def hyena_filter_spectrum(L, w1, b1, freq, w2, b2, w3):
    f32 = jnp.float32
    t = jnp.linspace(0.0, 1.0, L, dtype=f32)[:, None]
    w = 2.0 * math.pi * jnp.arange(L, dtype=f32)[:, None] / L
    bands = jnp.linspace(1e-4, HY_BANDS - 1, HY_BANDS, dtype=f32)[None, :]
    z = jnp.concatenate([t, jnp.cos(bands * w), -jnp.sin(bands * w)], axis=-1)
    h = jnp.sin(freq[0].astype(f32) * (z @ w1.astype(f32) + b1.astype(f32)))
    h = jnp.sin(freq[1].astype(f32) * (h @ w2.astype(f32) + b2.astype(f32)))
    h = (h @ w3.astype(f32)).reshape(L, 2, HY_ORDER, D_MODEL)
    deltas = jnp.abs(jnp.linspace(math.log(HY_TARGET) / HY_FAST_DECAY, math.log(HY_TARGET) / HY_SLOW_DECAY,
                                  D_MODEL, dtype=f32))
    h = h * (jnp.exp(-t * deltas[None, :]) + HY_MOD_SHIFT)[:, None, None, :]
    h_fwd, h_bwd = h[:, 0], h[:, 1]
    k_full = jnp.concatenate([h_fwd, jnp.zeros((1, HY_ORDER, D_MODEL), f32), h_bwd[1:][::-1]], axis=0)
    k_full = k_full / (jnp.sum(jnp.abs(k_full), axis=0, keepdims=True) + EPS)
    return jnp.fft.rfft(k_full, n=2 * L, axis=0)

def fft_longconv(u, kf, skip):
    L = u.shape[1]
    u32 = u.astype(jnp.float32)
    y = jnp.fft.irfft(jnp.fft.rfft(u32, n=2 * L, axis=1) * kf[None], n=2 * L, axis=1)[:, :L]
    return (y + u32 * skip.astype(jnp.float32)).astype(u.dtype)

def hyena_mixer(h, w_in, b_in, conv_w, conv_b, fw1, fb1, ffreq, fw2, fb2, fw3, skip, w_out):
    B, L, _ = h.shape
    p = h @ w_in + b_in
    p = lax.conv_general_dilated(p, conv_w.astype(p.dtype)[:, None, :], window_strides=(1,),
                                 padding=[(HY_SHORT // 2, HY_SHORT // 2)],
                                 dimension_numbers=('NWC', 'WIO', 'NWC'),
                                 feature_group_count=3 * D_MODEL) + conv_b
    v, x1, x2 = jnp.split(p, 3, axis=-1)
    kf = hyena_filter_spectrum(L, fw1, fb1, ffreq, fw2, fb2, fw3)
    z = x1 * fft_longconv(v, kf[:, 0], skip[0])
    z = x2 * fft_longconv(z, kf[:, 1], skip[1])
    return z @ w_out

def hier_moe(h, w_grp, b_grp, w_rt, b_rt, w_gate, w_up, w_down):
    B, L, D = h.shape
    t = h.reshape(B * L, D)
    n = t.shape[0]
    g_prob = jax.nn.softmax((t @ w_grp + b_grp).astype(jnp.float32), axis=-1)
    g_w, g_i = lax.top_k(g_prob, 1)
    e_logits = (t @ w_rt + b_rt).astype(jnp.float32).reshape(n, N_GROUPS, EXPERTS_PER_GROUP)
    e_logits = e_logits[jnp.arange(n), g_i[:, 0]]
    e_w, e_i = lax.top_k(jax.nn.softmax(e_logits, axis=-1), TOP_K)
    weights = e_w / jnp.sum(e_w, axis=-1, keepdims=True) * g_w
    ids = g_i * EXPERTS_PER_GROUP + e_i
    gates = jnp.sum(jax.nn.one_hot(ids, N_EXPERTS, dtype=jnp.float32) * weights[..., None], axis=1).astype(h.dtype)
    hg = jnp.einsum('nd,edf->nef', t, w_gate)
    hu = jnp.einsum('nd,edf->nef', t, w_up)
    y = jnp.einsum('nef,efd->nd', jax.nn.silu(hg) * hu * gates[:, :, None], w_down)
    return y.reshape(B, L, D)

def setup_inputs(seed: int = 0) -> dict:
    key = jax.random.key(seed)
    ks = jax.random.split(key, 64)
    counter = [0]

    def nrm(shape, scale=1.0):
        k = ks[counter[0]]
        counter[0] += 1
        return jax.random.normal(k, shape, jnp.float32) * scale

    def gain(shape):
        return 1.0 + nrm(shape, 0.05)

    D = D_MODEL
    NA = N_ATTN_LAYERS
    NH = N_HYENA_LAYERS
    return {
        'x_prompt': nrm((BATCH, SEQ, D)),
        'x_sample': nrm((DEC_BATCH, DEC_SEQ, D)),
        'cache_mla_ckv': nrm((DEC_BATCH, NA, PAST_LEN, KV_RANK)),
        'cache_mla_krope': nrm((DEC_BATCH, NA, PAST_LEN, ROPE_DIM)),
        'cache_na_k': nrm((DEC_BATCH, NA, PAST_LEN, NA_HEADS, NA_HEAD_DIM)),
        'cache_na_v': nrm((DEC_BATCH, NA, PAST_LEN, NA_HEADS, NA_HEAD_DIM)),
        'c': nrm((DEC_BATCH, D)),
        'c_ctx': nrm((D,)),
        'ada_w': nrm((DEPTH, D, 6 * D), 0.5 * D ** -0.5),
        'ada_b': nrm((DEPTH, 6 * D), 0.02),
        'norm_mix': gain((DEPTH, D)),
        'norm_ffn': gain((DEPTH, D)),
        'attn_w_in': nrm((NA, D, ATTN_IN), D ** -0.5),
        'mla_q_norm': gain((NA, Q_RANK)),
        'mla_kv_norm': gain((NA, KV_RANK)),
        'mla_w_q_up': nrm((NA, Q_RANK, MLA_HEADS * QK_DIM), Q_RANK ** -0.5),
        'mla_w_kv_up': nrm((NA, KV_RANK, MLA_HEADS * (NOPE_DIM + V_DIM)), KV_RANK ** -0.5),
        'mla_q_gain': gain((NA, QK_DIM)),
        'mla_k_gain': gain((NA, QK_DIM)),
        'na_q_gain': gain((NA, NA_HEAD_DIM)),
        'na_k_gain': gain((NA, NA_HEAD_DIM)),
        'na_rpb': nrm((NA, NA_HEADS, 2 * NA_KH - 1, 2 * NA_KW - 1), 0.5),
        'attn_w_out': nrm((NA, ATTN_OUT, D), ATTN_OUT ** -0.5),
        'hy_w_in': nrm((NH, D, 3 * D), D ** -0.5),
        'hy_b_in': nrm((NH, 3 * D), 0.02),
        'hy_conv_w': nrm((NH, HY_SHORT, 3 * D), HY_SHORT ** -0.5),
        'hy_conv_b': nrm((NH, 3 * D), 0.02),
        'hy_filt_w1': nrm((NH, HY_EMB, HY_FF), HY_EMB ** -0.5),
        'hy_filt_b1': nrm((NH, HY_FF), 0.1),
        'hy_filt_freq': 1.0 + nrm((NH, 2, HY_FF), 0.1),
        'hy_filt_w2': nrm((NH, HY_FF, HY_FF), HY_FF ** -0.5),
        'hy_filt_b2': nrm((NH, HY_FF), 0.1),
        'hy_filt_w3': nrm((NH, HY_FF, 2 * HY_ORDER * D), HY_FF ** -0.5),
        'hy_skip': nrm((NH, HY_ORDER, D), 0.5),
        'hy_w_out': nrm((NH, D, D), D ** -0.5),
        'moe_w_group': nrm((DEPTH, D, N_GROUPS), D ** -0.5),
        'moe_b_group': nrm((DEPTH, N_GROUPS), 0.01),
        'moe_w_router': nrm((DEPTH, D, N_EXPERTS), D ** -0.5),
        'moe_b_router': nrm((DEPTH, N_EXPERTS), 0.01),
        'moe_w_gate': nrm((DEPTH, N_EXPERTS, D, D_EXPERT), D ** -0.5),
        'moe_w_up': nrm((DEPTH, N_EXPERTS, D, D_EXPERT), D ** -0.5),
        'moe_w_down': nrm((DEPTH, N_EXPERTS, D_EXPERT, D), D_EXPERT ** -0.5),
    }

def reference(x_prompt, x_sample, cache_mla_ckv, cache_mla_krope, cache_na_k, cache_na_v, c, c_ctx,
              ada_w, ada_b, norm_mix, norm_ffn,
              attn_w_in, mla_q_norm, mla_kv_norm, mla_w_q_up, mla_w_kv_up, mla_q_gain, mla_k_gain,
              na_q_gain, na_k_gain, na_rpb, attn_w_out,
              hy_w_in, hy_b_in, hy_conv_w, hy_conv_b, hy_filt_w1, hy_filt_b1, hy_filt_freq,
              hy_filt_w2, hy_filt_b2, hy_filt_w3, hy_skip, hy_w_out,
              moe_w_group, moe_b_group, moe_w_router, moe_b_router, moe_w_gate, moe_w_up, moe_w_down):
    mla_scale = QK_DIM ** -0.5
    na_scale = NA_HEAD_DIM ** -0.5

    def attn_params(a):
        return (attn_w_in[a], mla_q_norm[a], mla_kv_norm[a], mla_w_q_up[a], mla_w_kv_up[a],
                mla_q_gain[a], mla_k_gain[a], na_q_gain[a], na_k_gain[a])

    def hyena_params(j):
        return (hy_w_in[j], hy_b_in[j], hy_conv_w[j], hy_conv_b[j], hy_filt_w1[j], hy_filt_b1[j],
                hy_filt_freq[j], hy_filt_w2[j], hy_filt_b2[j], hy_filt_w3[j], hy_skip[j], hy_w_out[j])

    def merge_heads(o_mla, o_na, a):
        B, L = o_mla.shape[:2]
        return jnp.concatenate([o_mla.reshape(B, L, -1), o_na.reshape(B, L, -1)], axis=-1) @ attn_w_out[a]

    def channel_mixer(x, l, shift, scale, gate):
        h = rmsnorm(x, norm_ffn[l]) * (1 + scale) + shift
        return x + gate * hier_moe(h, moe_w_group[l], moe_b_group[l], moe_w_router[l], moe_b_router[l],
                                   moe_w_gate[l], moe_w_up[l], moe_w_down[l])

    xp = x_prompt
    ckv_list, krope_list, nk_list, nv_list = [], [], [], []
    for l in range(DEPTH):
        sh1, sc1, g1, sh2, sc2, g2 = adaln(c_ctx[None, :], ada_w[l], ada_b[l])
        h = rmsnorm(xp, norm_mix[l]) * (1 + sc1) + sh1
        if l % 2 == 0:
            a = l // 2
            q, k, v, ckv, krope, nq, nk, nv = attn_in_proj(h, *attn_params(a))
            out = merge_heads(blocked_attention(q, k, v, mla_scale), blocked_attention(nq, nk, nv, na_scale), a)
            ckv_list.append(ckv)
            krope_list.append(krope)
            nk_list.append(nk)
            nv_list.append(nv)
        else:
            out = hyena_mixer(h, *hyena_params(l // 2))
        xp = channel_mixer(xp + g1 * out, l, sh2, sc2, g2)
    y_prompt = xp
    new_mla_ckv = jnp.stack(ckv_list, axis=1)
    new_mla_krope = jnp.stack(krope_list, axis=1)
    new_na_k = jnp.stack(nk_list, axis=1)
    new_na_v = jnp.stack(nv_list, axis=1)

    xs = x_sample
    for l in range(DEPTH):
        sh1, sc1, g1, sh2, sc2, g2 = adaln(c, ada_w[l], ada_b[l])
        h = rmsnorm(xs, norm_mix[l]) * (1 + sc1) + sh1
        if l % 2 == 0:
            a = l // 2
            q, k, v, _, _, nq, nk, nv = attn_in_proj(h, *attn_params(a))
            q = axial_rope(q)
            k = axial_rope(k)
            k_ctx, v_ctx = mla_expand(cache_mla_ckv[:, a], cache_mla_krope[:, a], mla_w_kv_up[a], mla_k_gain[a])
            o_mla = blocked_attention(q, jnp.concatenate([k, k_ctx], axis=1),
                                      jnp.concatenate([v, v_ctx], axis=1), mla_scale)
            o_na = neighbourhood_attention(nq, nk, nv, cache_na_k[:, a], cache_na_v[:, a], na_rpb[a])
            out = merge_heads(o_mla, o_na, a)
        else:
            out = hyena_mixer(h, *hyena_params(l // 2))
        xs = channel_mixer(xs + g1 * out, l, sh2, sc2, g2)
    y_sample = xs

    return (y_prompt, y_sample, new_mla_ckv, new_mla_krope, new_na_k, new_na_v)


_drawn_inputs = setup_inputs


def setup_inputs(seed=0):
    import zlib

    import numpy as np

    out = dict(_drawn_inputs(seed))
    spreads = {}
    factors = {'cache_mla_ckv': 3.701,
     'cache_mla_krope': 5.052,
     'cache_na_k': 2.742,
     'mla_q_norm': 8.0,
     'mla_q_gain': 8.0,
     'mla_k_gain': 8.0,
     'na_q_gain': 8.0,
     'na_rpb': 39.784,
     'hy_b_in': 8.0,
     'hy_conv_b': 8.0,
     'hy_filt_b1': 6.845,
     'hy_filt_freq': 8.0,
     'hy_filt_b2': 6.671,
     'moe_b_group': 15.252,
     'moe_b_router': 17.045}
    for name, (base, spread) in spreads.items():
        noise = np.random.default_rng([zlib.crc32(name.encode()), seed]).standard_normal(out[name].shape)
        drawn = base * np.exp(spread * noise) if base else spread * noise
        out[name] = jnp.asarray(drawn.astype(out[name].dtype))
    for name, factor in factors.items():
        out[name] = (out[name] * factor).astype(out[name].dtype)
    return out
```

```python
import math
from contextlib import ExitStack

import numpy as np

import concourse.bass as bass
from concourse import mybir

F32 = mybir.dt.float32
I32 = mybir.dt.int32
ALU = mybir.AluOpType
ACT = mybir.ActivationFunctionType
AX = mybir.AxisListType.X

P = 128
D = 1024
KC = D // P
SEQ, DEC = 128, 256
T = (SEQ + DEC) // P
NTOK = T * P
PAST = 128
NH = 8
QR, KVR, NOPE, ROPE, VD = 384, 128, 64, 32, 64
QK = NOPE + ROPE
NAD = 64
NAW = NH * NAD
WIN0 = QR + KVR + ROPE
GRID_W, ROWS = 64, DEC // 64
RPB_Y, RPB_X = 15, 31
FF = 64
EMB = 17
NG, EPG = 4, 8
NE = NG * EPG
DE = 256
EPS = 1e-6
NEG = -1e30
M = 32
SLOTS = 2 * NTOK
MAXSTEPS = SLOTS // M + NE
MAXPER = NTOK // M

MSLOT = 4608
ESLOT = 6144
RING = 0
RW = RING + 3 * MSLOT
XO = RING + 4 * ESLOT
HO = XO + T * D
HTO = HO + T * D
MODO = HTO + T * D
WORK = MODO + 6 * D
CONST = WORK + 11200
TAB = 644
COLO = CONST + TAB
CTO = COLO + 120
MROWO = CTO + 256
STO = MROWO + 768
TOTAL = STO + 260
DFT = 2560


def table():
    t = np.zeros((P, TAB), np.float32)
    t[:, 0:128] = np.eye(P)
    t[:, 128:256] = np.triu(np.ones((P, P)), 1)
    t[:, 256:384] = 1.0
    t[:, 384:416] = np.tile(np.eye(M), (4, 1))
    t[:NE, 416:448] = np.triu(np.ones((NE, NE)), 1)
    t[:NE, 448:480] = np.eye(NE)
    quarter = ROPE // 4
    inv = 10000.0 ** (-np.arange(quarter, dtype=np.float32) / quarter)
    tok = np.arange(DEC)
    for i, pos in enumerate((tok // GRID_W, tok % GRID_W)):
        ang = pos.astype(np.float32)[:, None] * inv[None].astype(np.float32)
        for tile in range(2):
            a = ang[tile * P:(tile + 1) * P]
            for half in range(2):
                o = tile * 64 + i * 16 + half * 8
                t[:, 480 + o:488 + o] = np.cos(a)
                t[:, 512 + o:520 + o] = np.sin(a) * (-1.0 if half == 0 else 1.0)
    t[:, 608:612] = np.arange(NG, 0, -1)
    t[:, 612:644] = np.arange(NE, 0, -1)
    return t


def dft_table():
    out = np.zeros((P, DFT), np.float32)
    o = 0
    for n in (DEC, SEQ):
        t = np.arange(n, dtype=np.float64)
        w = math.pi * (2 * t + 1) / (2 * n)
        c, s = np.cos(np.outer(t, w)), -np.sin(np.outer(t, w))
        for m in (c, s, c.T / n, s.T / n):
            k = n // P
            out[:, o:o + k * n] = m.reshape(k, P, n).transpose(1, 0, 2).reshape(P, k * n)
            o += k * n
    return out


def filter_positions():
    z, win = [], []
    deltas = np.abs(np.linspace(math.log(1e-2) / 0.3, math.log(1e-2) / 1.5, D, dtype=np.float32))
    for n in (SEQ, DEC):
        t = np.linspace(0.0, 1.0, n, dtype=np.float32)[:, None]
        w = (2.0 * math.pi * np.arange(n, dtype=np.float32)[:, None] / n).astype(np.float32)
        b = np.linspace(1e-4, 7, 8, dtype=np.float32)[None]
        z.append(np.concatenate([t, np.cos(b * w), -np.sin(b * w)], -1))
        win.append(np.exp(-t * deltas[None]) + np.float32(0.05))
    zt = np.concatenate(z, 0).T.astype(np.float32)
    return np.ascontiguousarray(zt), np.concatenate(win, 0).astype(np.float32)


class Signal:

    def __init__(self, sem):
        self.sem, self.count = sem, 0

    def by(self, ins, i):
        assert i == self.count, (i, self.count)
        self.count += 1
        ins.then_inc(self.sem, 1)

    def at(self, eng, i):
        eng.wait_ge(self.sem, i + 1)


class Chain:

    def __init__(self, eng, sem):
        self.eng, self.sem, self.n = eng, sem, 0

    def __call__(self, ins):
        self.n += 1
        ins.then_inc(self.sem, 1)
        self.eng.wait_ge(self.sem, self.n)


def build(nc, a, stage=99):
    ctx = ExitStack()
    with ctx:
        sb = ctx.enter_context(nc.sbuf_tensor("arena", [P, TOTAL], F32))
        ps = ctx.enter_context(nc.psum_tensor("banks", [P, 8, 512], F32))
        mod_d = nc.dram_tensor("mod_rows", (2, 2, 6 * D), F32).ap()
        y_d = [nc.dram_tensor(f"expert_rows{l}", (SLOTS + M, D), F32).ap() for l in range(2)]
        names = {}

        def sig(name):
            if name not in names:
                names[name] = Signal(ctx.enter_context(nc.semaphore(name)))
            return names[name]

        def sem(name):
            return ctx.enter_context(nc.semaphore(name))

        def v(off, *dims):
            n = int(np.prod(dims))
            ap = sb[:, off:off + n]
            if len(dims) == 2:
                return ap.rearrange("p (a b) -> p a b", a=dims[0])
            if len(dims) == 3:
                return ap.rearrange("p (a b c) -> p a b c", a=dims[0], b=dims[1])
            if len(dims) == 4:
                return ap.rearrange("p (a b c d) -> p a b c d", a=dims[0], b=dims[1], c=dims[2])
            return ap

        def bc(ap, n, at=1):
            dims = [list(x) for x in ap.ap]
            dims.insert(at, [0, n])
            return bass.AP(ap.tensor, ap.offset, dims)

        def rows(dram, off, n):
            return bass.AP(dram.tensor, off, [[0, P], [1, n]])

        x = v(XO, T, D)
        h = v(HO, T, KC, P)
        hT = v(HTO, KC, NTOK)
        mod = v(MODO, 2, 2, D)
        gate = v(MODO + 4 * D, 2, D)
        tab = v(CONST, TAB)
        ident, upper, ones = tab[:, 0:128], tab[:, 128:256], tab[:, 256:384]
        sel = tab[:, 384:416]
        upE, idE = tab[0:NE, 416:448], tab[0:NE, 448:480]
        first4, first32 = tab[:, 608:612], tab[:, 612:644]
        col = v(COLO, 120)
        cT = v(CTO, KC, 32)
        mrow = v(MROWO, 6, P)
        st = v(STO, 260)
        half_ = st[:, 0:8]
        msq, rstd = st[:, 8:16], st[:, 16:24]
        lat_ms, lat_rs = st[:, 24:40].rearrange("p (t c) -> p t c", c=4), st[:, 40:56].rearrange("p (t c) -> p t c", c=4)
        hms, hrs = st[:, 56:72].rearrange("p (b h) -> p b h", b=2), st[:, 72:88].rearrange("p (b h) -> p b h", b=2)
        negmax, rsum = st[:, 88:96], st[:, 96:104]
        wtok = st[:, 104:112]
        ppos = st[:, 112:120].bitcast(I32)

        def item(n, *dims):
            return v(RING + (n % 3) * MSLOT, *dims)

        def expert(s):
            o = RING + s * ESLOT
            gu = v(o, 2, KC, DE)
            return gu, v(o + 2 * KC * DE, 2, D)

        QT, KT = v(WORK, NH, NTOK), v(WORK + 3072, NH, NTOK + PAST)
        NQT, NKT = v(WORK + 7168, 4, NTOK), v(WORK + 8704, 4, NTOK + PAST)
        V = v(MODO, 4, D)
        bias = v(RW, 2, NH, ROWS, GRID_W)
        LT = v(RW + 4096, 4, NTOK + PAST)
        NB = v(RW + 6144, 2, NH * QK)
        cnk = v(RW + 7680, NAW)
        PB = v(RW + 8192, 2, 3, P)
        PTS = v(RW + 8960, 2, 3, P)
        tmp = v(RW + 8192, 2, 512)
        qn, kvn = v(RW + 9728, QR), v(RW + 10112, KVR)
        nqg, nkg = v(RW + 10240, NAD), v(RW + 10304, NAD)
        qg, kg = v(RW + 10368, QK), v(RW + 10464, QK)
        lat = v(HO, 3, WIN0)
        cin = v(HO + 3 * WIN0, KVR + ROPE)
        sq = v(HO + 1792, 768)
        rt = v(HO + 2560, 2, NH, 32)
        OT = hT
        gain = v(WORK + 10176, D)
        junk = v(WORK + D, D)

        items0 = ([("ada", 0, n) for n in range(4)] + [("win", i) for i in range(4)] + [("up",)]
                  + [("ada", 0, n) for n in range(4, 12)] + [("ada", 1, n) for n in range(12)]
                  + [("out", 0), ("out", 1)])
        items1 = [("hyin", i) for i in range(6)] + [("w3",), ("hyout", 0), ("hyout", 1)]
        items = items0 + items1
        number = {k: n for n, k in enumerate(items)}
        ndma = {"ada": 2, "up": 2}
        loads = [0, 0, 0]
        landed = {}
        for n, k in enumerate(items):
            loads[n % 3] += 16 * ndma.get(k[0], 1)
            landed[k] = loads[n % 3]
        item_loaded = [sem(f"item_loaded{i}") for i in range(3)]
        expert_loaded = [sem(f"expert_loaded{i}") for i in range(4)]
        expert_free = [sem(f"expert_free{i}") for i in range(4)]
        mod_stored = [sem(f"mod_stored{i}") for i in range(8)]
        gathered = [sem(f"gathered{i}") for i in range(6)]
        step = {n: [sem(f"{n}{l}") for l in range(2)] for n in (
            "moe_x", "moe_pg", "moe_g", "moe_pt", "moe_e", "moe_dve", "moe_a", "moe_py", "moe_y", "moe_stored")}
        in_const, in_x, in_c, in_bias, in_gains, in_ctx, in_ctxv = (
            sem(n) for n in ("in_const", "in_x", "in_c", "in_bias", "in_gains", "in_ctx", "in_ctxv"))
        sb_loaded, gate_loaded, gain_loaded, route_loaded = (
            sem(n) for n in ("sb_loaded", "gate_loaded", "gain_loaded", "route_loaded"))
        in_dft, in_win, in_hy, in_rows = (sem(n) for n in ("in_dft", "in_win", "in_hy", "in_rows"))
        out_sem, pool_out = sem("outputs_stored"), sem("pool_out")
        n_out = [0]

        place, owner, turn = {}, [None] * 8, [0]

        def open_(pe, kind, i, freed_by):
            b = turn[0] % 8
            turn[0] += 1
            for name, j in owner[b] or ():
                sig(name).at(pe, j)
            owner[b] = freed_by
            place[kind, i] = b
            return ps[:, b, :]

        def close(mm, kind, i):
            sig("psum_" + kind).by(mm, i)

        def read(eng, kind, i):
            sig("psum_" + kind).at(eng, i)
            return ps[:, place[kind, i], :]

        units = ([("nq", t) for t in range(3)] + [("nk", t) for t in range(3)]
                 + [("q", t) for t in range(3)] + [("k", t) for t in range(4)])
        proj, uT = {}, {}
        n = 0
        for kind, t in units[:6] + [("nv", t) for t in range(3)] + units[6:]:
            for j in range(2 if kind in "qk" else 1):
                proj[kind, t, j] = n
                n += 1
        n = 0
        for kind, t in units + [("ck", 3)]:
            for j in range(2 if kind in "qk" else 1):
                uT[kind, t, j] = n
                n += 1
        chunks = [(0, n) for n in range(4, 12)] + [(1, n) for n in range(12)]
        at_unit = {7: chunks[0], 9: chunks[1]}
        at_head = {int(2.6 * n) + 1: c for n, c in enumerate(chunks[2:])}
        heads = [(kind, t, hd) for kind in range(2) for t in range(T) for hd in range(NH)]
        NU = len(heads)
        MLA_SCALE = QK ** -0.5

        def nkeys(t):
            return 1 if t == 0 else 3

        def router_off():
            return WORK + 6400

        def steps_of(eng, e):
            return (eng.value_load(tbi[0:1, bass.ds(e, 1)], min_val=1, max_val=MAXPER),
                    eng.value_load(tbi[0:1, bass.ds(e + NE, 1)], min_val=0, max_val=MAXSTEPS))

        XS = v(WORK, KC, 800)
        WR = v(WORK + 6400, KC, 36)
        brt = v(WORK + 6688, 36)
        logit = v(WORK + 6724, T, 36)
        rw = v(WORK + 6832, 768)
        iota = v(WORK + 7600, 768)
        xcur = v(WORK + 8368, KC, M)
        gsb = v(WORK + 8624, 2, 2, P)
        ysb = v(WORK + 9136, DE)
        ex, e1, e2 = (v(WORK + 9392 + 64 * i, 2, M) for i in range(3))
        aT = v(WORK + 9584, 2, M)
        tbi = v(WORK + 9648, 96).bitcast(I32)
        cc = v(WORK, 4 * P)
        pref = v(WORK + 9744, 96)
        PH = v(MODO, T, SLOTS)
        YG = [v(HO, T, D), v(HTO, T, D)]
        X1, X2T = v(WORK, T, D), v(WORK + 3072, 8, 386)
        KF = v(WORK + 6160, 6, 512)
        Z1 = v(WORK + 9232, T, 512)
        H2T = v(WORK + 10768, NTOK)
        VT = v(RW, T, D)
        dft = v(RW + 3072, DFT)
        PF, PM = v(RW + 5632, T, 512), v(RW + 7168, T, 512)
        AB = [v(o, 512) for o in (RW + 8704, RW + 9216, HO + 2560, *(RING + i * MSLOT + 4096 for i in range(3)))]
        TM = v(RW + 9728, 2, 512)
        YF = v(MODO, 6, 512)
        RN = v(MODO + 3072, 2, 512)
        PP, CV = v(HO, 2, 388), v(HO + 776, 2, 388)
        WN, SK = v(HO, T, 512), v(HO + 1536, 2, 512)
        Z2T = hT
        hrow = v(RW + 5632, P)
        zT, f1, f2, w1, w2, fcol = (v(MODO + o, n) for o, n in (
            (0, NTOK), (384, NTOK), (768, NTOK), (1152, FF), (1216, FF), (1280, 4)))
        f3 = v(MODO + 1536, NTOK)
        c256, n256 = dft[:, 0:512].rearrange("p (k j) -> p k j", k=2), dft[:, 512:1024].rearrange("p (k j) -> p k j", k=2)
        ct256, nt256 = dft[:, 1024:1536].rearrange("p (k j) -> p k j", k=2), dft[:, 1536:2048].rearrange("p (k j) -> p k j", k=2)
        c128, n128, ct128, nt128 = (dft[:, 2048 + 128 * i:2176 + 128 * i].rearrange("p (k j) -> p k j", k=1) for i in range(4))
        spectra = [((1, 2), c256, n256, 0), ((1, 2), c256, n256, 1), ((0,), c128, n128, 0)]

        block = ctx.enter_context(nc.Block())

        @block.tensor
        def _(pe):
            def mm(out, lhsT, rhs, start=True, stop=True):
                return pe.matmul(out, lhsT, rhs, start=start, stop=stop, skip_group_check=True)

            def arrived(k):
                pe.wait_ge(item_loaded[number[k] % 3], landed[k])
                return number[k]

            def used(ins, k):
                sig("item_used").by(ins, number[k])

            def ada(l, n):
                i = arrived(("ada", l, n))
                w = item(i, KC, 512)
                brow = v(RING + (i % 3) * MSLOT + 4096, 512)
                o = open_(pe, "ada", l * 12 + n, [("ada_row", l * 12 + n)])
                for k in range(KC):
                    for g in range(4):
                        mm(o[32 * g:32 * g + 32, 0:P], cT[:, k, :], w[:, k, g * P:(g + 1) * P], k == 0, False)
                for g in range(4):
                    last = mm(o[32 * g:32 * g + 32, 0:P], ones[0:1, 0:32], brow[0:1, g * P:(g + 1) * P], False, True)
                close(last, "ada", l * 12 + n)

            def transposes(u, tiles=range(T)):
                for t in tiles:
                    sig("h").at(pe, u * 3 + t)
                    for j in range(2):
                        i = (u * 3 + t) * 2 + j
                        o = open_(pe, "hT", i, [("hT", i)])
                        for k in range(4):
                            last = pe.transpose(o[:, k * P:(k + 1) * P], h[:, t, 4 * j + k, :], ident)
                        close(last, "hT", i)

            def out_proj(l, kind):
                for j in range(2):
                    w = item(arrived((kind, j)), KC, 512)
                    for t in range(T):
                        i = l * 6 + j * 3 + t
                        o = open_(pe, "out", i, [("xmix", i)])
                        for k in range(KC):
                            last = mm(o, (OT if l == 0 else Z2T)[:, k, t * P:(t + 1) * P], w[:, k, :], k == 0, k == KC - 1)
                        close(last, "out", i)

            def attention():
                n0 = arrived(("win", 0))
                w = item(n0, KC, WIN0)
                for t in range(T):
                    sig("hT").at(pe, t * 2 + 1)
                    for kind, c0, c1 in (("qlat", 0, QR), ("kvr", QR, WIN0)):
                        o = open_(pe, kind, t, [("lat", t)])
                        for k in range(KC):
                            last = mm(o[:, 0:c1 - c0], hT[:, k, t * P:(t + 1) * P], w[:, k, c0:c1], k == 0, k == KC - 1)
                        close(last, kind, t)

                def produce(kind, t):
                    if kind in ("nq", "nk", "nv"):
                        w = item(arrived(("win", {"nq": 1, "nk": 2, "nv": 3}[kind])), KC, 512)
                        i = proj[kind, t, 0]
                        o = open_(pe, "proj", i, [("nv", t)] if kind == "nv" else [("normed", units.index((kind, t)))])
                        for k in range(KC):
                            last = mm(o, hT[:, k, t * P:(t + 1) * P], w[:, k, :], k == 0, k == KC - 1)
                        close(last, "proj", i)
                        return
                    base = RING + (arrived(("up",)) % 3) * MSLOT
                    wq, wkv = v(base, 3, NH * QK), v(base + 2304, NH * 2 * NOPE)
                    sig("latT").at(pe, t)
                    for j in range(2):
                        i = proj[kind, t, j]
                        n = units.index((kind, t))
                        if kind == "q":
                            o = open_(pe, "proj", i, [("normed", n)])
                            for c in range(3):
                                last = mm(o[:, 0:384], LT[:, c, t * P:(t + 1) * P], wq[:, c, j * 384:(j + 1) * 384], c == 0, c == 2)
                        else:
                            o = open_(pe, "proj", i, [("normed", n), ("vout", t)])
                            last = mm(o, LT[:, 3, t * P:(t + 1) * P], wkv[:, j * 512:(j + 1) * 512])
                        close(last, "proj", i)

                def turn_unit(kind, t):
                    if kind == "ck":
                        src, n = cnk, None
                        pe.wait_ge(in_ctx, 48)
                    else:
                        n = units.index((kind, t))
                        sig("normed").at(pe, n)
                        src = NB[:, n % 2, :]
                    for j in range(2 if kind in "qk" else 1):
                        i = uT[kind, t, j]
                        o = open_(pe, "uT", i, [("uT", i)])
                        for b in range(4):
                            if kind in "qk":
                                hd = 4 * j + b
                                last = pe.transpose(o[0:QK, b * P:(b + 1) * P], src[:, hd * QK:(hd + 1) * QK], ident)
                            else:
                                last = pe.transpose(o[:, b * P:(b + 1) * P], src[:, b * P:(b + 1) * P], ident)
                        close(last, "uT", i)

                def turn_latents(t):
                    o = open_(pe, "latT", t, [("latT", t)])
                    if t < T:
                        sig("lat").at(pe, t)
                        for c in range(4):
                            last = pe.transpose(o[:, c * P:(c + 1) * P], lat[:, t, c * P:(c + 1) * P], ident)
                    else:
                        last = pe.transpose(o[:, 3 * P:4 * P], cin[:, 0:KVR], ident)
                    close(last, "latT", t)

                produce("nq", 0)
                for n, (kind, t) in enumerate(units):
                    if n + 1 < len(units):
                        if units[n + 1] == ("q", 0):
                            for tt in range(T):
                                produce("nv", tt)
                            pe.wait_ge(in_ctx, 48)
                            for tt in range(4):
                                turn_latents(tt)
                        produce(*units[n + 1])
                    if n in at_unit:
                        ada(*at_unit[n])
                    turn_unit(kind, t)
                turn_unit("ck", 3)

                def scores(i):
                    kind, t, hd = heads[i]
                    if i == 0:
                        sig("uT").at(pe, uT["ck", 3, 0])
                        pe.wait_ge(in_ctxv, 16)
                    o = open_(pe, "S", i, [("expd", i)])
                    k0, k1 = (0, P) if t == 0 else (P, NTOK + PAST)
                    if kind == 0:
                        q, k = QT[0:QK, hd, t * P:(t + 1) * P], KT[0:QK, hd, k0:k1]
                    else:
                        r = 64 * (hd % 2)
                        q, k = NQT[r:r + 64, hd // 2, t * P:(t + 1) * P], NKT[r:r + 64, hd // 2, k0:k1]
                    close(mm(o[:, 0:k1 - k0], q, k), "S", i)

                def turn_probs(i):
                    o = open_(pe, "PT", i, [("PT", i)])
                    sig("prob").at(pe, i)
                    for b in range(nkeys(heads[i][1])):
                        last = pe.transpose(o[:, b * P:(b + 1) * P], PB[:, i % 2, b, :], ident)
                    close(last, "PT", i)

                def values(i):
                    kind, t, hd = heads[i]
                    if hd % 2 == 0:
                        open_(pe, "O", i // 2, [("OT", i // 2)])
                    o = ps[:, place["O", i // 2], :]
                    sig("PT").at(pe, i)
                    n = nkeys(t)
                    r = 64 * (hd % 2)
                    for b in range(n):
                        last = mm(o[r:r + 64, 0:P], V[:, 0 if t == 0 else 1 + b, kind * 512 + hd * 64:kind * 512 + hd * 64 + 64],
                                  PTS[:, i % 2, b, :], b == 0, b == n - 1)
                    sig("pv").by(last, i)

                for i in range(NU + 2):
                    if i < NU:
                        scores(i)
                    if 1 <= i <= NU:
                        turn_probs(i - 1)
                    if i >= 2:
                        values(i - 2)
                    if i in at_head:
                        ada(*at_head[i])

            def moe(l):
                u = 2 * l + 1
                transposes(u, (0,))
                o_logit = open_(pe, "logit", l, [("logit", l)])
                pe.wait_ge(route_loaded, 64 * (l + 1))
                for t in range(T):
                    if t + 1 < T:
                        transposes(u, (t + 1,))
                    sig("hT").at(pe, (u * 3 + t) * 2 + 1)
                    for k in range(KC):
                        last = mm(o_logit[:, t * 36:(t + 1) * 36], hT[:, k, t * P:(t + 1) * P], WR[:, k, :], k == 0, k == KC - 1)
                close(last, "logit", l)
                sig("choice").at(pe, l)
                both = v(WORK + 6832 + 480, T, NE)
                o = open_(pe, "rank", l, [("pos", l)])
                for t in range(T):
                    for s in range(t + 1):
                        last = mm(o[:, t * NE:(t + 1) * NE], upper if s == t else ones, both[:, s, :], s == 0, s == t)
                close(last, "rank", l)
                o = open_(pe, "count", l, [("count", l)])
                for t in range(T):
                    last = mm(o[0:NE, 0:P], both[:, t, :], ones, t == 0, t == T - 1)
                close(last, "count", l)
                sig("count").at(pe, l)
                o = open_(pe, "pref", l, [("pref", l)])
                mm(o[:, 0:32], cc[0:NE, P:2 * P], idE)
                mm(o[:, 32:64], cc[0:NE, P:2 * P], upE)
                close(mm(o[:, 64:96], cc[0:NE, 0:P], upE), "pref", l)
                sig("onehot").at(pe, l)
                for k in range(KC):
                    for j, (c0, c1) in enumerate(((0, 512), (512, SLOTS))):
                        i = (l * KC + k) * 2 + j
                        o = open_(pe, "xs", i, [("xs_a" if j == 0 else "xs_d", l * KC + k)])
                        for t in range(T):
                            last = mm(o[:, 0:c1 - c0], h[:, t, k, :], PH[:, t, c0:c1], t == 0, t == T - 1)
                        close(last, "xs", i)
                pg, pt, py = (open_(pe, n, l, [("moe_end", l)]) for n in ("pg", "pt", "py"))
                s_ = {k: q[l] for k, q in step.items()}
                pe.sem_inc(s_["moe_pg"], 1)

                def down_product(g, down):
                    pe.wait_ge(s_["moe_a"], g)
                    pe.wait_ge(s_["moe_y"], g)
                    for f in range(2):
                        for q in range(4):
                            last = mm(py[32 * q:32 * q + 32, 0:DE], aT[:, f, :], down[:, f, q * DE:(q + 1) * DE], f == 0, f == 1)
                    last.then_inc(s_["moe_py"], 1)

                def one_step(g, slot, before):
                    gu = expert(slot)[0]
                    pe.wait_ge(s_["moe_x"], g + 1)
                    for k in range(KC):
                        c = slice(32 * (k % 4), 32 * (k % 4) + 32)
                        last = mm(pg[c, :].rearrange("p (i n) -> p i n", i=2), xcur[:, k, :], gu[:, :, k, :], k < 4, k >= 4)
                    last.then_inc(s_["moe_pg"], 1)
                    if before is not None:
                        down_product(g, expert(before)[1])
                    pe.wait_ge(s_["moe_g"], g + 1)
                    for c in range(4):
                        last = mm(pt[:, c * M:(c + 1) * M], gsb[:, c // 2, c % 2, :], sel)
                    last.then_inc(s_["moe_pt"], 1)

                def one_expert(r, s, before):
                    n, b = steps_of(pe, r * 4 + s)
                    pe.wait_ge(expert_loaded[s], (r + 1) * 48 + l * 48 * (NE // 4))
                    one_step(b, s, before)
                    with pe.If_ne(pe.to_reg(n), 1):
                        with pe.Fori(1, n) as j:
                            one_step(b + j, s, s)

                for s in range(4):
                    one_expert(0, s, s - 1 if s else None)
                with pe.Fori(1, NE // 4) as r:
                    for s in range(4):
                        one_expert(r, s, (s - 1) % 4)
                n, b = steps_of(pe, NE - 1)
                down_product(n + b, expert(3)[1])

            def hyena():
                pe.wait_ge(in_rows, 80)
                o = open_(pe, "col", 0, [("col", 0)])
                close(pe.transpose(o[:, 0:120], hrow[0:120, :], ident[0:120, 0:120]), "col", 0)
                pe.wait_ge(in_hy, 16 * 7)
                o = open_(pe, "net", 0, [("net", 0)])
                close(mm(o[0:FF, 0:NTOK], w1[0:EMB, :], zT[0:EMB, :]), "net", 0)
                sig("sin").at(pe, 0)
                o = open_(pe, "net", 1, [("net", 1)])
                close(mm(o[0:FF, 0:NTOK], w2[0:FF, :], f2[0:FF, :]), "net", 1)
                for t in range(T):
                    sig("hT").at(pe, (2 * 3 + t) * 2 + 1)

                def turn_channels(ct):
                    sig("cv").at(pe, ct)
                    o = open_(pe, "cvT", ct, [("cvT", ct)])
                    for t in range(T):
                        c0 = 1 if t == 0 else 2 + t * P
                        last = pe.transpose(o[:, t * P:(t + 1) * P], CV[:, ct % 2, c0:c0 + P], ident)
                    close(last, "cvT", ct)

                for ct in range(24):
                    w = item(arrived(("hyin", ct // 4)), KC, 512)
                    o = open_(pe, "hp", ct, [("hp", ct)])
                    for k in range(KC):
                        last = mm(o[:, 0:NTOK], w[:, k, (ct % 4) * P:(ct % 4 + 1) * P], hT[:, k, :], k == 0, k == KC - 1)
                    close(last, "hp", ct)
                    if 1 <= ct <= 16:
                        turn_channels(ct - 1)

                n3 = arrived(("w3",))
                w3 = item(n3, 4096)
                pe.wait_ge(in_dft, 16)
                sig("sin").at(pe, 1)

                def taps(b):
                    ch, od = b // 2, b % 2
                    for t in range(T):
                        for dr in range(2):
                            i = (b * 3 + t) * 2 + dr
                            o = open_(pe, "filt", i, [("filt", i)])
                            c = (dr * 2 + od) * D + ch * 512
                            close(mm(o, H2T[0:FF, t * P:(t + 1) * P], w3[0:FF, c:c + 512]), "filt", i)

                def filter_spectra(b):
                    for g in range(2):
                        tiles = (0,) if g == 0 else (1, 2)
                        o = open_(pe, "nrm", b * 2 + g, [("nrm", b * 2 + g)])
                        for t in tiles:
                            for dr in range(2):
                                i = (b * 3 + t) * 2 + dr
                                sig("abs").at(pe, i)
                                last = mm(o, ones, AB[i % 6], t == tiles[0] and dr == 0, t == tiles[-1] and dr == 1)
                                sig("abs_used").by(last, i)
                    for s, (tiles, cm, nm, jt) in enumerate(spectra):
                        for im in range(2):
                            i = b * 6 + s * 2 + im
                            o = open_(pe, "K", i, [("K", i)])
                            sig("fpm").at(pe, b * 3 + tiles[-1])
                            m = (cm, nm)[im]
                            for q, t in enumerate(tiles):
                                last = mm(o, m[:, q, jt * P:(jt + 1) * P], (PF, PM)[im][:, t, :], q == 0, q == len(tiles) - 1)
                            close(last, "K", i)

                def signal_spectra(b):
                    ch, od = b // 2, b % 2
                    for s, (tiles, cm, nm, jt) in enumerate(spectra):
                        for im in range(2):
                            i = b * 6 + s * 2 + im
                            o = open_(pe, "U", i, [("prod", b * 3 + s)])
                            m = (cm, nm)[im]
                            for q, t in enumerate(tiles):
                                if od == 0:
                                    if b == 0:
                                        sig("cvT").at(pe, 15)
                                    src = VT[:, t, ch * 512:(ch + 1) * 512]
                                else:
                                    sig("z1").at(pe, ch * 3 + t)
                                    src = Z1[:, t, :]
                                last = mm(o, m[:, q, jt * P:(jt + 1) * P], src, q == 0, q == len(tiles) - 1)
                            close(last, "U", i)

                def inverse(b):
                    ch, od = b // 2, b % 2
                    sig("prod").at(pe, b * 3 + 2)
                    if od == 0:
                        for t in range(T):
                            o = open_(pe, "Y", ch * 3 + t, [("z1", ch * 3 + t)])
                            js, cm, nm, q = ((2,), ct128, nt128, 0) if t == 0 else ((0, 1), ct256, nt256, t - 1)
                            for a_, s in enumerate(js):
                                mm(o, cm[:, a_, q * P:(q + 1) * P], YF[:, 2 * s, :], a_ == 0, False)
                                last = mm(o, nm[:, a_, q * P:(q + 1) * P], YF[:, 2 * s + 1, :], False, a_ == len(js) - 1)
                            close(last, "Y", ch * 3 + t)
                        return
                    for c in range(4):
                        i = ch * 4 + c
                        o = open_(pe, "YT", i, [("z2", i)])
                        cs = slice(c * P, (c + 1) * P)
                        mm(o[:, 0:P], YF[:, 4, cs], ct128[:, 0, :], True, False)
                        mm(o[:, 0:P], YF[:, 5, cs], nt128[:, 0, :], False, True)
                        for s in range(2):
                            mm(o[:, P:NTOK], YF[:, 2 * s, cs], ct256[:, s, :], s == 0, False)
                            last = mm(o[:, P:NTOK], YF[:, 2 * s + 1, cs], nt256[:, s, :], False, s == 1)
                        close(last, "YT", i)

                taps(0)
                for b in range(4):
                    filter_spectra(b)
                    signal_spectra(b)
                    if b < 3:
                        taps(b + 1)
                    inverse(b)
                sig("z2").at(pe, 7)

            pe.wait_ge(in_const, 16)
            sig("cT").at(pe, 0)
            for n in range(4):
                ada(0, n)
            transposes(0)
            if stage >= 1:
                attention()
                sig("OT").at(pe, NU // 2 - 1)
                out_proj(0, "out")
            if stage >= 2:
                moe(0)
            if stage >= 3:
                transposes(2)
                hyena()
                out_proj(1, "hyout")
            if stage >= 4:
                moe(1)

        @block.vector
        def _(dve):
            link = Chain(dve, sem("dve_chain"))

            def tt(o, p, q, op):
                return dve.tensor_tensor(o, p, q, op)

            def ada_row(m):
                o = read(dve, "ada", m)
                if m >= 6:
                    g = [0, 0, 0, 0, 1, 1, 2, 2, 2, 2, 3, 3][(m - 6) % 12] + 4 * ((m - 6) // 12)
                    dve.wait_ge(mod_stored[g], 64)
                sig("ada_row").by(dve.tensor_copy(mrow[:, m % 6, :], o[:, 0:P]), m)

            def scales(u):
                dve.wait_ge(gain_loaded, 16 * (u + 1))
                dve.wait_ge(sb_loaded, 32 * (u + 1))
                for g in range(2):
                    link(dve.scalar_tensor_tensor(mod[:, g, 1, :], mod[:, g, 1, :], 1.0, gain, ALU.add, ALU.mult))

            def norm(u, t):
                sig("rstd").at(dve, u * 3 + t)
                g = min(t, 1)
                ht = h[:, t].rearrange("p k q -> p q k")
                xt = x[:, t, :].rearrange("p (q k) -> p q k", k=KC)
                link(dve.scalar_tensor_tensor(ht, xt, rstd[:, t:t + 1], mod[:, g, 1, :].rearrange("p (q k) -> p q k", k=KC),
                                              ALU.mult, ALU.mult))
                sig("h").by(tt(ht, ht, mod[:, g, 0, :].rearrange("p (q k) -> p q k", k=KC), ALU.add), u * 3 + t)

            def residual(l):
                dve.wait_ge(gate_loaded, 32 * (2 * l + 1))
                for j in range(2):
                    for t in range(T):
                        i = l * 6 + j * 3 + t
                        o = read(dve, "out", i)
                        c = slice(j * 512, (j + 1) * 512)
                        link(tt(tmp[:, i % 2, :], o, gate[:, min(t, 1), c], ALU.mult))
                        sig("xmix").by(tt(x[:, t, c], x[:, t, c], tmp[:, i % 2, :], ALU.add), i)
                        if j == 1 and t >= 1:
                            norm(2 * l + 1, t - 1)
                norm(2 * l + 1, T - 1)

            def attention():
                link(dve.tensor_scalar(nqg, nqg, NAD ** -0.5, None, ALU.mult))
                for t in range(T):
                    q, kv = read(dve, "qlat", t), read(dve, "kvr", t)
                    sig("lat_rs").at(dve, t)
                    dve.scalar_tensor_tensor(lat[:, t, 0:QR], q[:, 0:QR], lat_rs[:, t, 0:1], qn, ALU.mult, ALU.mult)
                    dve.scalar_tensor_tensor(lat[:, t, QR:QR + KVR], kv[:, 0:KVR], lat_rs[:, t, 1:2], kvn, ALU.mult, ALU.mult)
                    sig("lat").by(dve.tensor_copy(lat[:, t, QR + KVR:WIN0], kv[:, KVR:KVR + ROPE]), t)
                for n, (kind, t) in enumerate(units):
                    if n - 1 in at_unit:
                        l, c = at_unit[n - 1]
                        ada_row(l * 12 + c)
                    b = n % 2
                    sig("sq").at(dve, n)
                    w = NOPE if kind != "q" else QK
                    red = dve.tensor_reduce(hms[:, b, :], sq[:, 0:NH * w].rearrange("p (h w) -> p h w", h=NH), AX, ALU.add)
                    if kind == "k":
                        link(red)
                        red = dve.tensor_scalar(hms[:, b, :], hms[:, b, :], lat_ms[:, t, 2:3], None, ALU.add)
                    sig("hms").by(red, n)
                    sig("hrs").at(dve, n)
                    if n >= 2:
                        pk, pt = units[n - 2]
                        sig("psum_uT").at(dve, uT[pk, pt, 1 if pk in "qk" else 0])
                    d = NB[:, b, :]
                    if n == 5:
                        dve.wait_ge(out_sem, 16)
                    if kind in ("nq", "nk"):
                        o = read(dve, "proj", proj[kind, t, 0])
                        dv = d[:, 0:NAW].rearrange("p (h w) -> p h w", h=NH)
                        link(tt(dv, o.rearrange("p (h w) -> p h w", h=NH), bc(hrs[:, b, :], NAD, 2), ALU.mult))
                        sig("normed").by(tt(dv, dv, bc(nqg if kind == "nq" else nkg, NH, 1), ALU.mult), n)
                        continue
                    dv = d.rearrange("p (h w) -> p h w", h=NH)
                    if kind == "k":
                        sig("vout").at(dve, t)
                    for j in range(2):
                        o = read(dve, "proj", proj[kind, t, j])
                        hs = slice(4 * j, 4 * j + 4)
                        if kind == "q":
                            ins = tt(dv[:, hs, :], o[:, 0:384].rearrange("p (h w) -> p h w", h=4), bc(hrs[:, b, hs], QK, 2), ALU.mult)
                        else:
                            ins = tt(dv[:, hs, 0:NOPE], o.rearrange("p (h w) -> p h w", h=4)[:, :, 0:NOPE], bc(hrs[:, b, hs], NOPE, 2), ALU.mult)
                    if kind == "k":
                        kr = lat[:, t, QR + KVR:WIN0] if t < T else cin[:, KVR:KVR + ROPE]
                        ins = tt(dv[:, :, NOPE:QK], bc(kr, NH, 1), bc(hrs[:, b, :], ROPE, 2), ALU.mult)
                    link(ins)
                    ins = tt(dv, dv, bc(qg if kind == "q" else kg, NH, 1), ALU.mult)
                    if t in (1, 2):
                        link(ins)
                        r = dv[:, :, NOPE:QK]
                        o = 480 + (t - 1) * 64
                        cos, sin = tab[:, o:o + 32], tab[:, o + 32:o + 64]
                        tt(rt[:, 0], r, bc(cos, NH, 1), ALU.mult)
                        for half in range(2):
                            dst = rt[:, 1].rearrange("p h (c s e) -> p h c s e", c=2, s=2)[:, :, :, half]
                            src = r.rearrange("p h (c s e) -> p h c s e", c=2, s=2)[:, :, :, 1 - half]
                            sn = sin.rearrange("p (c s e) -> p c s e", c=2, s=2)[:, :, half]
                            ins = tt(dst, src, bc(sn, NH, 1), ALU.mult)
                        link(ins)
                        ins = tt(r, rt[:, 0], rt[:, 1], ALU.add)
                    sig("normed").by(ins, n)

                for i in range(NU + 2):
                    if 1 <= i <= NU:
                        j = i - 1
                        n = nkeys(heads[j][1])
                        sig("expd").at(dve, j)
                        c = rsum[:, j % 8:j % 8 + 1]
                        link(dve.reciprocal(c, c))
                        pb = PB[:, j % 2, 0:n, :]
                        sig("prob").by(dve.tensor_scalar(pb, pb, c, None, ALU.mult), j)
                    if i < NU:
                        kind, t, hd = heads[i]
                        n = P if t == 0 else 3 * P
                        o = read(dve, "S", i)
                        if kind == 1 and t > 0:
                            if hd == 0:
                                sig("bias").at(dve, 1)
                            link(tt(o[:, 0:DEC], o[:, 0:DEC], bias[:, t - 1, hd].rearrange("p r c -> p (r c)"), ALU.add))
                        c = negmax[:, i % 8:i % 8 + 1]
                        link(dve.reduce_max(c, o[:, 0:n], AX))
                        sig("negmax").by(dve.tensor_scalar(c, c, -(MLA_SCALE if kind == 0 else 1.0), None, ALU.mult), i)
                    if i in at_head:
                        l, n = at_head[i]
                        ada_row(l * 12 + n)

            def moe(l):
                both = v(WORK + 6832 + 480, T, NE)
                o = read(dve, "logit", l)
                dve.wait_ge(route_loaded, 64 * (l + 1))
                ov = o[:, 0:108].rearrange("p (t c) -> p t c", t=T)
                ins = tt(logit, ov, bc(brt, T, 1), ALU.add)
                sig("logit").by(ins, l)
                sig("logit").at(dve, l)
                G, E = logit[:, :, 0:NG], logit[:, :, NG:36]
                sc = v(WORK + 6832, 48)
                gm, gs, km, m1, m2, gw = (sc[:, 3 * i:3 * i + 3] for i in range(6))
                dm = sc[:, 20:23]
                gx = sc[:, 24:36].rearrange("p (t c) -> p t c", t=T)
                key = sc[:, 36:48].rearrange("p (t c) -> p t c", t=T)
                big = [v(WORK + 6832 + 48 + 96 * i, T, NE) for i in range(4)]
                EL, oh1, oh2, kb = big
                link(dve.reduce_max(gm, G, AX))
                link(tt(gx, G, bc(gm, NG, 2), ALU.subtract))
                sig("gx").by(tt(key, G, bc(gm, NG, 2), ALU.is_equal), l)
                sig("gx").at(dve, l)
                link(tt(key, key, bc(first4, T, 1), ALU.mult))
                link(dve.reduce_max(km, key, AX))
                link(tt(key, key, bc(km, NG, 2), ALU.is_equal))
                link(dve.tensor_scalar(key, key, 1.0, -NEG, ALU.subtract, ALU.mult))
                link(tt(EL, E, bass.AP(key.tensor, key.offset, [list(key.ap[0]), [1, 12], [0, EPG]]), ALU.add))

                def best(mx, oh):
                    link(dve.reduce_max(mx, EL, AX))
                    link(tt(kb, EL, bc(mx, NE, 2), ALU.is_equal))
                    link(tt(kb, kb, bc(first32, T, 1), ALU.mult))
                    link(dve.reduce_max(km, kb, AX))
                    link(tt(oh, kb, bc(km, NE, 2), ALU.is_equal))

                best(m1, oh1)
                link(dve.scalar_tensor_tensor(EL, oh1, NEG, EL, ALU.mult, ALU.add))
                best(m2, oh2)
                link(tt(dm, m2, m1, ALU.subtract))
                sig("choice").by(tt(both, oh1, oh2, ALU.add), l)
                sig("gexp").at(dve, l)
                link(dve.tensor_reduce(gs, gx, AX, ALU.add))
                link(dve.reciprocal(gw, gs))
                wt = [wtok[:, 0:3], wtok[:, 3:6]]
                link(dve.tensor_scalar(gs, dm, 1.0, None, ALU.add))
                link(dve.reciprocal(gs, gs))
                link(tt(wt[0], gs, gw, ALU.mult))
                link(tt(wt[1], wt[0], dm, ALU.mult))
                o = read(dve, "count", l)
                ci = cc[0:NE, 2 * P:3 * P].bitcast(I32)
                dve.tensor_copy(cc[0:NE, 0:P], o[0:NE, 0:P])
                link(dve.tensor_scalar(ci, o[0:NE, 0:P], float(M - 1), None, ALU.add))
                link(dve.tensor_scalar(ci, ci, int(math.log2(M)), None, ALU.logical_shift_right))
                sig("count").by(dve.tensor_scalar(cc[0:NE, P:2 * P], ci, 1.0, None, ALU.max), l)
                o = read(dve, "pref", l)
                link(dve.tensor_copy(pref, o[:, 0:96]))
                sig("pref").by(dve.tensor_copy(tbi, pref), l)
                o = read(dve, "rank", l)
                rv = o[:, 0:T * NE].rearrange("p (t e) -> p t e", t=T)
                link(tt(EL, rv, bc(pref[:, 64:96], T, 1), ALU.add))
                pos = v(WORK + 6832 + 576, 12)
                for q, oh in enumerate((oh1, oh2)):
                    link(tt(both, oh, EL, ALU.mult))
                    link(dve.tensor_reduce(pos[:, q * 3:q * 3 + 3], both, AX, ALU.add))
                sig("pos").by(dve.tensor_copy(ppos[:, 0:6], pos[:, 0:6]), l)
                sig("iota").at(dve, l)
                for t in range(T):
                    link(dve.tensor_scalar(PH[:, t, :], iota, pos[:, t:t + 1], None, ALU.is_equal))
                    ins = dve.scalar_tensor_tensor(PH[:, t, :], iota, pos[:, 3 + t:4 + t], PH[:, t, :], ALU.is_equal, ALU.add)
                    if t == T - 1:
                        sig("onehot").by(ins, l)
                for k in range(KC):
                    o = read(dve, "xs", (l * KC + k) * 2 + 1)
                    sig("xs_d").by(dve.tensor_copy(XS[:, k, 512:SLOTS], o[:, 0:SLOTS - 512]), l * KC + k)
                pt = ps[:, place["pt", l], :]
                s_ = {k: q[l] for k, q in step.items()}
                ptv = pt[:, 0:4 * M].rearrange("p (u f m) -> p u f m", u=2, f=2)
                with dve.Fori(0, NE) as e:
                    n, b = steps_of(dve, e)
                    with dve.Fori(0, n) as j:
                        dve.wait_ge(s_["moe_e"], b + j + 1)
                        dve.tensor_scalar(e1, ex, 1.0, None, ALU.add).then_inc(s_["moe_dve"], 1)
                        dve.wait_ge(s_["moe_dve"], (b + j) * 3 + 1)
                        dve.reciprocal(e2, e1).then_inc(s_["moe_dve"], 1)
                        dve.wait_ge(s_["moe_dve"], (b + j) * 3 + 2)
                        tt(e1, ptv[:, 0], e2, ALU.mult).then_inc(s_["moe_dve"], 1)
                        dve.wait_ge(s_["moe_dve"], (b + j) * 3 + 3)
                        tt(aT, ptv[:, 1], e1, ALU.mult).then_inc(s_["moe_a"], 1)
                if l == 0:
                    scales(2)
                dve.wait_ge(gate_loaded, 32 * (2 * l + 2))
                for t in range(T):
                    sig("weighted").at(dve, l * 3 + t)
                    y1, y2 = YG[0][:, t, :], YG[1][:, t, :]
                    link(dve.scalar_tensor_tensor(y1, y2, wtok[:, 3 + t:4 + t], y1, ALU.mult, ALU.add))
                    link(tt(y1, y1, gate[:, min(t, 1), :], ALU.mult))
                    sig("xffn").by(tt(x[:, t, :], x[:, t, :], y1, ALU.add), l * 3 + t)
                    if l == 0 and t >= 1:
                        norm(2, t - 1)
                if l == 0:
                    norm(2, T - 1)

            def hyena():
                sig("col").by(dve.tensor_copy(col, read(dve, "col", 0)[:, 0:120]), 0)
                TWO_PI = 2 * math.pi
                c1 = float(np.float32(6.28125))
                c2 = float(np.float32(TWO_PI - c1))
                c3 = TWO_PI - c1 - c2
                dve.wait_ge(in_hy, 16 * 7)
                for i in range(2):
                    o = read(dve, "net", i)
                    dst, k = f1[0:FF, :], f3[0:FF, :]
                    ins = dve.tensor_scalar(dst, o[0:FF, 0:NTOK], fcol[0:FF, 2 * i:2 * i + 1], fcol[0:FF, 2 * i + 1:2 * i + 2], ALU.add, ALU.mult)
                    sig("net").by(ins, i)
                    sig("net").at(dve, i)
                    link(dve.tensor_scalar(k, dst, 1.0 / TWO_PI, 12582912.0, ALU.mult, ALU.add))
                    link(dve.tensor_scalar(k, k, 12582912.0, None, ALU.subtract))
                    for c in (c1, c2, c3):
                        link(dve.scalar_tensor_tensor(dst, k, -c, dst, ALU.mult, ALU.add))
                    lim = 3.1415925
                    sig("arg").by(dve.tensor_scalar(dst, dst, lim, -lim, ALU.min, ALU.max), i)
                    sig("sin").at(dve, i)
                for b in range(2):
                    pads = bass.AP(PP.tensor, PP[:, b, 0:1].offset, [list(PP.ap[0]), [129, 2]])
                    dve.memset(pads, 0.0)
                    link(dve.memset(PP[:, b, 386:387], 0.0))
                for ct in range(24):
                    sig("hp").at(dve, ct)
                    if 2 <= ct < 18:
                        sig("psum_cvT").at(dve, ct - 2)
                    p = PP[:, ct % 2, :]
                    d = CV[:, ct % 2, 1:386] if ct < 16 else X2T[:, ct - 16, 0:385]
                    w0, w1_, w2_ = (col[:, 48 + 24 * i + ct:49 + 24 * i + ct] for i in range(3))
                    link(dve.tensor_scalar(d, p[:, 1:386], w1_, col[:, 24 + ct:25 + ct], ALU.mult, ALU.add))
                    link(dve.scalar_tensor_tensor(d, p[:, 0:385], w0, d, ALU.mult, ALU.add))
                    sig("cv").by(dve.scalar_tensor_tensor(d, p[:, 2:387], w2_, d, ALU.mult, ALU.add), ct)
                def windowed(b):
                    dve.wait_ge(in_win, 80 * (b // 2 + 1))
                    if b > 0:
                        sig("psum_K").at(dve, (b - 1) * 6 + 5)
                    for t in range(T):
                        fw, bw, i = PF[:, t, :], TM[:, t % 2, :], (b * 3 + t) * 2
                        sig("filt").by(tt(fw, read(dve, "filt", i), WN[:, t, :], ALU.mult), i)
                        sig("filt").by(tt(bw, read(dve, "filt", i + 1), WN[:, t, :], ALU.mult), i + 1)
                        sig("filt").at(dve, i + 1)
                        if t < 2:
                            link(dve.memset(bw[0:1, :], 0.0))
                        sig("fb").by(tt(PM[:, t, :], fw, bw, ALU.subtract), b * 3 + t)
                        sig("abs").at(dve, i + 1)
                        sig("fpm").by(tt(fw, fw, bw, ALU.add), b * 3 + t)

                windowed(0)
                for b in range(4):
                    ch, od = b // 2, b % 2
                    hs = slice(ch * 512, (ch + 1) * 512)
                    for g in range(2):
                        sig("abs_used").at(dve, (b * 3 + 2 * g) * 2 + 1)
                        o = ps[:, place["nrm", b * 2 + g], :]
                        sig("nrm").by(dve.tensor_scalar(RN[:, g, :], o, EPS, None, ALU.add), b * 2 + g)
                        sig("nrm").at(dve, b * 2 + g)
                        link(dve.reciprocal(RN[:, g, :], RN[:, g, :]))
                    for s in range(3):
                        g = 0 if s == 2 else 1
                        for im in range(2):
                            i = b * 6 + s * 2 + im
                            d = KF[:, s * 2 + im, :]
                            sig("K").by(tt(d, read(dve, "K", i), RN[:, g, :], ALU.mult), i)
                            if im == 0:
                                sig("K").at(dve, i)
                                link(tt(d, d, SK[:, od, :], ALU.add))
                    for s in range(3):
                        sig("K").at(dve, b * 6 + s * 2 + 1)
                        ur, ui = read(dve, "U", b * 6 + s * 2), read(dve, "U", b * 6 + s * 2 + 1)
                        kr, ki = KF[:, 2 * s, :], KF[:, 2 * s + 1, :]
                        yr, yi = YF[:, 2 * s, :], YF[:, 2 * s + 1, :]
                        tt(yr, ur, kr, ALU.mult)
                        link(tt(TM[:, 0, :], ui, ki, ALU.mult))
                        tt(yr, yr, TM[:, 0, :], ALU.subtract)
                        tt(yi, ur, ki, ALU.mult)
                        link(tt(TM[:, 1, :], ui, kr, ALU.mult))
                        sig("prod").by(tt(yi, yi, TM[:, 1, :], ALU.add), b * 3 + s)
                    if b < 3:
                        windowed(b + 1)
                    if od == 0:
                        for t in range(T):
                            i = ch * 3 + t
                            sig("z1").by(tt(Z1[:, t, :], read(dve, "Y", i), X1[:, t, hs], ALU.mult), i)
                    else:
                        for c in range(4):
                            i = ch * 4 + c
                            o = read(dve, "YT", i)
                            tt(Z2T[:, i, 0:P], o[:, 0:P], X2T[:, i, 0:P], ALU.mult)
                            sig("z2").by(tt(Z2T[:, i, P:NTOK], o[:, P:NTOK], X2T[:, i, P + 1:NTOK + 1], ALU.mult), i)

            dve.memset(cT, 0.0)
            cv_ = v(WORK, 2, KC)
            ce = v(WORK + 16, 2, KC)
            dve.wait_ge(in_c, 32)
            sig("cexp").at(dve, 0)
            link(dve.tensor_scalar(ce, ce, 1.0, None, ALU.add))
            link(dve.reciprocal(ce, ce))
            sig("cT").by(tt(cT[:, :, 0:2].rearrange("p k r -> p r k"), cv_, ce, ALU.mult), 0)
            for n in range(4):
                ada_row(n)
            scales(0)
            for t in range(T):
                norm(0, t)
            if stage >= 1:
                dve.wait_ge(in_gains, 16 * 6)
                attention()
                scales(1)
                residual(0)
            if stage >= 2:
                moe(0)
            if stage >= 3:
                hyena()
                scales(3)
                residual(1)
            if stage >= 4:
                moe(1)

        @block.scalar
        def _(act):
            link = Chain(act, sem("act_chain"))

            def store(dst, src):
                n_out[0] += 16
                act.dma_start(dst, src).then_inc(out_sem, 16)

            def squares(u):
                for t in range(T):
                    if u == 0:
                        act.wait_ge(in_x, 32)
                    elif u % 2 == 1:
                        sig("xmix").at(act, (u // 2) * 6 + 3 + t)
                    else:
                        sig("xffn").at(act, (u // 2 - 1) * 3 + t)
                    if t:
                        sig("ms").at(act, u * 3 + t - 1)
                    sig("ms").by(act.activation(junk, x[:, t, :], ACT.Square, scale=D ** -0.5, accum_out=msq[:, t:t + 1]), u * 3 + t)

            def hT_out(u):
                for t in range(T):
                    for j in range(2):
                        i = (u * 3 + t) * 2 + j
                        o = read(act, "hT", i)
                        sig("hT").by(act.activation(hT[:, 4 * j:4 * j + 4, t * P:(t + 1) * P],
                                                    o.rearrange("p (k t) -> p k t", k=4), ACT.Copy), i)

            def attention():
                for t in range(T):
                    q, kv = read(act, "qlat", t), read(act, "kvr", t)
                    if t:
                        sig("lat_ms").at(act, t - 1)
                    act.activation(sq[:, 0:QR], q[:, 0:QR], ACT.Square, scale=QR ** -0.5, accum_out=lat_ms[:, t, 0:1])
                    act.activation(sq[:, QR:QR + KVR], kv[:, 0:KVR], ACT.Square, scale=KVR ** -0.5, accum_out=lat_ms[:, t, 1:2])
                    sig("lat_ms").by(act.activation(sq[:, 512:512 + ROPE], kv[:, KVR:KVR + ROPE], ACT.Square, scale=QK ** -0.5,
                                                    accum_out=lat_ms[:, t, 2:3]), t)
                act.wait_ge(in_ctx, 48)
                sig("lat_ms").at(act, T - 1)
                act.activation(sq[:, 512:512 + ROPE], cin[:, KVR:KVR + ROPE], ACT.Square, scale=QK ** -0.5, accum_out=lat_ms[:, 3, 2:3])

                def square_unit(n):
                    kind, t = units[n]
                    if n >= 1:
                        sig("hms").at(act, n - 1)
                    if kind in ("nq", "nk"):
                        o = read(act, "proj", proj[kind, t, 0])
                        sig("sq").by(act.activation(sq[:, 0:NAW], o, ACT.Square, scale=NAD ** -0.5), n)
                        return
                    for j in range(2):
                        o = read(act, "proj", proj[kind, t, j])
                        if kind == "q":
                            ins = act.activation(sq[:, 384 * j:384 * (j + 1)], o[:, 0:384], ACT.Square, scale=QK ** -0.5)
                        else:
                            ins = act.activation(sq[:, 256 * j:256 * (j + 1)].rearrange("p (h w) -> p h w", h=4),
                                                 o.rearrange("p (h w) -> p h w", h=4)[:, :, 0:NOPE], ACT.Square, scale=QK ** -0.5)
                    sig("sq").by(ins, n)
                    if kind == "k":
                        for j in range(2):
                            o = read(act, "proj", proj[kind, t, j])
                            ins = act.activation(V[:, t, 256 * j:256 * (j + 1)].rearrange("p (h w) -> p h w", h=4),
                                                 o.rearrange("p (h w) -> p h w", h=4)[:, :, NOPE:], ACT.Copy)
                        sig("vout").by(ins, t)

                def turned(kind, t):
                    for j in range(2 if kind in "qk" else 1):
                        i = uT[kind, t, j]
                        o = read(act, "uT", i).rearrange("p (b t) -> p b t", b=4)
                        ts_ = slice(t * P, (t + 1) * P)
                        if kind in "qk":
                            dst, o = (QT if kind == "q" else KT)[0:QK, 4 * j:4 * j + 4, ts_], o[0:QK]
                        else:
                            dst = (NQT if kind == "nq" else NKT)[:, :, ts_]
                        sig("uT").by(act.activation(dst, o, ACT.Copy), i)

                square_unit(0)
                for n, (kind, t) in enumerate(units):
                    if n + 1 < len(units):
                        if units[n + 1] == ("q", 0):
                            for tt_ in range(T):
                                o = read(act, "proj", proj["nv", tt_, 0])
                                sig("nv").by(act.activation(V[:, tt_, NAW:], o, ACT.Copy), tt_)
                            for tt_ in range(4):
                                o = read(act, "latT", tt_).rearrange("p (c t) -> p c t", c=4)
                                c0 = 0 if tt_ < T else 3
                                sig("latT").by(act.activation(LT[:, c0:4, tt_ * P:(tt_ + 1) * P], o[:, c0:4, :], ACT.Copy), tt_)
                        square_unit(n + 1)
                    turned(kind, t)
                    if (kind, t) == ("nk", 0):
                        store(a["new_na_k"].rearrange("b a t h d -> (b a t) (h d)"), NB[:, n % 2, 0:NAW])
                turned("ck", 3)
                sig("lat").at(act, 0)
                store(a["new_mla_ckv"].rearrange("b a t c -> (b a t) c"), lat[:, 0, QR:QR + KVR])
                store(a["new_mla_krope"].rearrange("b a t c -> (b a t) c"), lat[:, 0, QR + KVR:WIN0])
                store(a["new_na_v"].rearrange("b a t h d -> (b a t) (h d)"), V[:, 0, NAW:])

                for i in range(NU + 2):
                    if 1 <= i <= NU:
                        j = i - 1
                        n = nkeys(heads[j][1])
                        o = read(act, "PT", j)
                        if j >= 2:
                            sig("pv").at(act, j - 2)
                        sig("PT").by(act.activation(PTS[:, j % 2, 0:n, :], o[:, 0:n * P].rearrange("p (b k) -> p b k", b=n), ACT.Copy), j)
                    if i < NU:
                        kind, t, hd = heads[i]
                        n = nkeys(t)
                        sig("negmax").at(act, i)
                        if i >= 2:
                            sig("psum_PT").at(act, i - 2)
                        o = read(act, "S", i)
                        sig("expd").by(act.activation(PB[:, i % 2, 0:n, :].rearrange("p b k -> p (b k)"), o[:, 0:n * P], ACT.Exp,
                                                      bias=negmax[:, i % 8:i % 8 + 1], scale=MLA_SCALE if kind == 0 else 1.0,
                                                      accum_out=rsum[:, i % 8:i % 8 + 1]), i)
                    if i >= 2 and i % 2 == 1:
                        j = i - 2
                        kind, t, hd = heads[j]
                        sig("pv").at(act, j)
                        sig("OT").by(act.activation(OT[:, kind * 4 + hd // 2, t * P:(t + 1) * P],
                                                    ps[:, place["O", j // 2], 0:P], ACT.Copy), j // 2)

            def moe(l):
                sc = v(WORK + 6832, 48)
                sig("gx").at(act, l)
                act.activation(sc[:, 24:36], sc[:, 24:36], ACT.Exp)
                sig("choice").at(act, l)
                sig("gexp").by(act.activation(sc[:, 20:23], sc[:, 20:23], ACT.Exp), l)
                for k in range(KC):
                    o = read(act, "xs", (l * KC + k) * 2)
                    sig("xs_a").by(act.activation(XS[:, k, 0:512], o, ACT.Copy), l * KC + k)
                pg, pt, py = (ps[:, place[n, l], :] for n in ("pg", "pt", "py"))
                s_ = {k: q[l] for k, q in step.items()}
                sig("pref").at(act, l)
                act.sem_inc(s_["moe_y"], 1)
                act.sem_inc(s_["moe_stored"], 16)

                def rows_out(g, row):
                    act.wait_ge(s_["moe_py"], g)
                    act.wait_ge(s_["moe_stored"], g * 16)
                    act.activation(ysb, py[:, 0:DE], ACT.Copy).then_inc(s_["moe_y"], 1)
                    act.wait_ge(s_["moe_y"], g + 1)
                    row = nc.s_assert_within(row, 0, SLOTS,
                                             skip_runtime_bounds_check_because="a step starts at a slot of its expert")
                    act.dma_start(y_d[l][bass.ds(row, M), :].rearrange("s (q c) -> q s c", q=4), ysb)\
                       .then_inc(s_["moe_stored"], 16)

                def one_step(g, row):
                    act.wait_ge(s_["moe_pg"], g + 2)
                    act.activation(gsb.rearrange("p i f q -> p i q f"),
                                   pg.rearrange("p (i q f) -> p i q f", i=2, f=2), ACT.Copy).then_inc(s_["moe_g"], 1)
                    act.wait_ge(s_["moe_pt"], g + 1)
                    act.activation(ex, pt[:, 0:2 * M].rearrange("p (f m) -> p f m", f=2), ACT.Exp, scale=-1.0).then_inc(s_["moe_e"], 1)
                    if row is not None:
                        rows_out(g, row)

                def first_row(e):
                    return act.value_load(tbi[0:1, bass.ds(e + 2 * NE, 1)], min_val=0, max_val=SLOTS)

                def last_row(e):
                    n, _ = steps_of(act, e)
                    return first_row(e) + (n - 1) * M

                def one_expert(r, s, peeled):
                    e = r * 4 + s
                    n, b = steps_of(act, e)
                    one_step(b, None if peeled else last_row(e - 1))
                    if not peeled:
                        act.sem_inc(expert_free[(s - 1) % 4], 1)
                    with act.If_ne(act.to_reg(n), 1):
                        o = first_row(e)
                        with act.Fori(1, n) as j:
                            one_step(b + j, o + (j - 1) * M)

                for s in range(4):
                    one_expert(0, s, s == 0)
                with act.Fori(1, NE // 4) as r:
                    for s in range(4):
                        one_expert(r, s, False)
                n, b = steps_of(act, NE - 1)
                rows_out(n + b, last_row(NE - 1))
                act.sem_inc(expert_free[3], 1)
                for t in range(T):
                    act.wait_ge(gathered[l * 3 + t], 32)
                    y1 = YG[0][:, t, :]
                    sig("weighted").by(act.activation(y1, y1, ACT.Copy, scale=wtok[:, t:t + 1]), l * 3 + t)
                act.activation(ex, ex, ACT.Copy).then_inc(sig("moe_end").sem, 1)

            def hyena():
                for i in range(2):
                    sig("arg").at(act, i)
                    dst = f2 if i == 0 else H2T
                    sig("sin").by(act.activation(dst[0:FF, 0:NTOK], f1[0:FF, :], ACT.Sin), i)
                sig("col").at(act, 0)

                def channels_out(ct):
                    o = read(act, "cvT", ct)
                    dst = (VT if ct < 8 else X1)[:, :, (ct % 8) * P:(ct % 8 + 1) * P]
                    sig("cvT").by(act.activation(dst, o[:, 0:NTOK].rearrange("p (t c) -> p t c", t=T), ACT.Copy), ct)

                for ct in range(24):
                    o = read(act, "hp", ct)
                    if ct >= 2:
                        sig("cv").at(act, ct - 2)
                    p = PP[:, ct % 2, :]
                    act.activation(p[:, 1:1 + P], o[:, 0:P], ACT.Identity, bias=col[:, ct:ct + 1])
                    sig("hp").by(act.activation(p[:, 130:386], o[:, P:NTOK], ACT.Identity, bias=col[:, ct:ct + 1]), ct)
                    if 1 <= ct <= 16:
                        channels_out(ct - 1)
                for b in range(4):
                    for t in range(T):
                        for dr in range(2):
                            i = (b * 3 + t) * 2 + dr
                            if dr == 0:
                                sig("fb").at(act, b * 3 + t)
                            if i >= 6:
                                sig("abs_used").at(act, i - 6)
                            src = PF[:, t, :] if dr == 0 else TM[:, t % 2, :]
                            sig("abs").by(act.activation(AB[i % 6], src, ACT.Abs), i)

            for g, n in enumerate(("c_ctx", "c")):
                src = a[n] if g == 0 else a[n].rearrange("b d -> (b d)")
                act.dma_start(v(WORK, 2, KC)[:, g, :], src.rearrange("(p k) -> p k", k=KC)).then_inc(in_c, 16)
            act.dma_start(tab, a["tab"]).then_inc(in_const, 16)
            act.dma_start(x[:, 0, :], a["x_prompt"].rearrange("b t d -> (b t) d")).then_inc(in_x, 16)
            act.dma_start(x[:, 1:3, :], a["x_sample"].rearrange("b (t p) d -> p (b t) d", p=P)).then_inc(in_x, 16)
            act.wait_ge(in_c, 32)
            sig("cexp").by(act.activation(v(WORK + 16, 2, KC), v(WORK, 2, KC), ACT.Exp, scale=-1.0), 0)
            if stage >= 1:
                for dst, nme, n in ((qn, "mla_q_norm", QR), (kvn, "mla_kv_norm", KVR), (nqg, "na_q_gain", NAD),
                                    (nkg, "na_k_gain", NAD), (qg, "mla_q_gain", QK), (kg, "mla_k_gain", QK)):
                    act.dma_start(dst, rows(a[nme], 0, n)).then_inc(in_gains, 16)
            squares(0)
            hT_out(0)
            if stage >= 1:
                attention()
            if stage >= 2:
                squares(1)
                hT_out(1)
                moe(0)
            if stage >= 3:
                squares(2)
                hT_out(2)
                hyena()
            if stage >= 4:
                squares(3)
                hT_out(3)
                moe(1)
            if stage < 4 and stage >= 1:
                for t in range(T):
                    if stage == 2:
                        sig("xffn").at(act, t)
                    else:
                        sig("xmix").at(act, (6 if stage == 3 else 0) + 3 + t)
                    store(a["dbg"][t], x[:, t, :])
            if stage >= 4:
                for t in range(T):
                    sig("xffn").at(act, 3 + t)
                    dst = a["y_prompt"].rearrange("b t d -> (b t) d") if t == 0 else \
                        a["y_sample"].rearrange("b (t p) d -> (b t) p d", p=P)[t - 1]
                    store(dst, x[:, t, :])
            act.wait_ge(out_sem, n_out[0])

        @block.gpsimd
        def _(pool):
            link = Chain(pool, sem("pool_chain"))

            def power(dst, src, n, name, i):
                link(pool.tensor_scalar(dst, src, EPS, None, ALU.add))
                sig(name).by(pool.tensor_tensor(dst, dst, half_[:, 0:n], ALU.pow), i)
                sig(name).at(pool, i)

            def moe(l):
                sig("h").at(pool, (2 * l + 1) * 3 + 2)
                link(pool.iota(iota.bitcast(I32), [[1, SLOTS]], base=0, channel_multiplier=0))
                sig("iota").by(pool.tensor_copy(iota, iota.bitcast(I32)), l)
                sig("iota").at(pool, l)
                link(pool.memset(XS[:, :, SLOTS:800], 0.0))
                sig("xs_a").at(pool, (l + 1) * KC - 1)
                sig("xs_d").at(pool, (l + 1) * KC - 1)
                s_ = {k: q[l] for k, q in step.items()}
                with pool.Fori(0, NE) as e:
                    n, b = steps_of(pool, e)
                    o = pool.value_load(tbi[0:1, bass.ds(e + 2 * NE, 1)], min_val=0, max_val=SLOTS)
                    with pool.Fori(0, n) as j:
                        first = nc.s_assert_within(o + j * M, 0, SLOTS,
                                                   skip_runtime_bounds_check_because="a step starts at a slot of its expert")
                        pool.wait_ge(s_["moe_pg"], b + j + 1)
                        pool.tensor_copy(xcur, XS[:, :, bass.ds(first, M)]).then_inc(s_["moe_x"], 1)
                n, b = steps_of(pool, NE - 1)
                sig("pos").at(pool, l)
                pool.wait_ge(s_["moe_stored"], (n + b + 1) * 16)
                link(pool.tensor_tensor(half_, half_, ones[:, 0:8], ALU.mult))
                for t in range(T):
                    for q in range(2):
                        pool.indirect_dma_start(YG[q][:, t, :], None, y_d[l][0:SLOTS, :],
                                                bass.IndirectOffsetOnAxis(ap=ppos[:, q * 3 + t:q * 3 + t + 1], axis=0))\
                            .then_inc(gathered[l * 3 + t], 16)

            link(pool.memset(half_, -0.5))

            def rms(u):
                for t in range(T):
                    sig("ms").at(pool, u * 3 + t)
                    power(rstd[:, t:t + 1], msq[:, t:t + 1], 1, "rstd", u * 3 + t)

            rms(0)
            if stage >= 1:
                sig("h").at(pool, 2)
                pool.dma_start(V[:, 3, NAW:], a["cache_na_v"].rearrange("b a t h d -> (b a t) (h d)")).then_inc(in_ctxv, 16)
                sig("psum_hT").at(pool, 5)
                for dst, nme in ((cin[:, 0:KVR], "cache_mla_ckv"), (cin[:, KVR:], "cache_mla_krope")):
                    pool.dma_start(dst, a[nme].rearrange("b a t c -> (b a t) c")).then_inc(in_ctx, 16)
                pool.dma_start(cnk, a["cache_na_k"].rearrange("b a t h d -> (b a t) (h d)")).then_inc(in_ctx, 16)
                for t in range(T):
                    sig("lat_ms").at(pool, t)
                    power(lat_rs[:, t, 0:2], lat_ms[:, t, 0:2], 2, "lat_rs", t)
                for n in range(len(units)):
                    sig("hms").at(pool, n)
                    power(hrs[:, n % 2, :], hms[:, n % 2, :], 8, "hrs", n)
                pool.wait_ge(in_bias, 16)
                for hf in range(2):
                    b = bias[64 * hf:64 * hf + 64].rearrange("p a b c d -> p (a b c) d")
                    link(pool.affine_select(out=b[:, :, 0:48], in_=b[:, :, 0:48], compare_op=ALU.is_ge, fill=NEG,
                                            base=8, pattern=[[0, 64], [1, 48]], channel_multiplier=-1))
                    sig("bias").by(pool.affine_select(out=b[:, :, 16:64], in_=b[:, :, 16:64], compare_op=ALU.is_ge, fill=NEG,
                                                      base=-9, pattern=[[0, 64], [-1, 48]], channel_multiplier=1), hf)
                    sig("bias").at(pool, hf)
            if stage >= 2:
                rms(1)
                moe(0)
            if stage >= 3:
                rms(2)
            if stage >= 4:
                rms(3)
                moe(1)

        @block.sync
        def _(sp):
            def load(k):
                n = number[k]
                if n >= 3:
                    wait_used(sp, items[n - 3])
                s = item_loaded[n % 3]
                if k[0] == "ada":
                    _, l, c = k
                    sp.dma_start(item(n, KC, 512), a["ada_w"][l].rearrange("(p k) n -> p k n", k=KC)[:, :, c * 512:(c + 1) * 512]).then_inc(s, 16)
                    o = RING + (n % 3) * MSLOT + 4096
                    sp.dma_start(sb[0:1, o:o + 512], a["ada_b"][l:l + 1, c * 512:(c + 1) * 512]).then_inc(s, 16)
                elif k[0] == "win":
                    c0, w = (0, WIN0) if k[1] == 0 else (WIN0 + NAW * (k[1] - 1), NAW)
                    sp.dma_start(item(n, KC, w), a["attn_w_in"][0].rearrange("(p k) n -> p k n", k=KC)[:, :, c0:c0 + w]).then_inc(s, 16)
                elif k[0] == "up":
                    sp.dma_start(item(n, 3, NH * QK), a["mla_w_q_up"][0].rearrange("(c p) n -> p c n", p=P)).then_inc(s, 16)
                    sp.dma_start(v(RING + (n % 3) * MSLOT + 2304, NH * 2 * NOPE), a["mla_w_kv_up"][0]).then_inc(s, 16)
                elif k[0] in ("out", "hyout"):
                    w = a["attn_w_out"] if k[0] == "out" else a["hy_w_out"]
                    sp.dma_start(item(n, KC, 512), w[0].rearrange("(c p) n -> p c n", p=P)[:, :, k[1] * 512:(k[1] + 1) * 512]).then_inc(s, 16)
                elif k[0] == "hyin":
                    sp.dma_start(item(n, KC, 512), a["hy_w_in"][0].rearrange("(p k) n -> p k n", k=KC)[:, :, k[1] * 512:(k[1] + 1) * 512]).then_inc(s, 16)
                elif k[0] == "w3":
                    sp.dma_start(item(n, 4096)[0:FF, :], a["hy_filt_w3"][0]).then_inc(s, 16)

            def wait_used(eng, k):
                if k[0] == "ada":
                    sig("psum_ada").at(eng, k[1] * 12 + k[2])
                elif k == ("win", 0):
                    sig("psum_kvr").at(eng, T - 1)
                elif k[0] == "win":
                    sig("psum_proj").at(eng, proj[("nq", "nk", "nv")[k[1] - 1], T - 1, 0])
                elif k[0] == "up":
                    sig("psum_proj").at(eng, proj["k", 3, 1])
                elif k[0] in ("out", "hyout"):
                    sig("psum_out").at(eng, (6 if k[0] == "hyout" else 0) + k[1] * 3 + 2)
                elif k[0] == "hyin":
                    sig("psum_hp").at(eng, k[1] * 4 + 3)
                elif k[0] == "w3":
                    sig("psum_filt").at(eng, 23)

            def store_mod(l, j):
                c0, n = ((0, 4), (4, 2), (6, 4), (10, 2))[j]
                m0 = l * 12 + c0
                sig("ada_row").at(sp, m0 + n - 1)
                dst = mod_d[l].rearrange("r (c g x) -> g r c x", c=12, g=4)
                for g in range(4):
                    sp.dma_start(dst[g, :, c0:c0 + n, :], mrow[32 * g:32 * g + 2, m0 % 6:m0 % 6 + n, :]).then_inc(mod_stored[l * 4 + j], 16)

            def load_mod(l, sub):
                u = 2 * l + sub
                sp.wait_ge(mod_stored[l * 4 + 2 * sub], 64)
                for g in range(2):
                    sp.dma_start(v(MODO + g * 2 * D, 2 * D), rows(mod_d, (l * 2 + g) * 6 * D + sub * 3 * D, 2 * D)).then_inc(sb_loaded, 16)
                src = a["norm_mix"] if sub == 0 else a["norm_ffn"]
                sp.dma_start(gain, rows(src, l * D, D)).then_inc(gain_loaded, 16)

            def load_gate(l, sub):
                sp.wait_ge(mod_stored[l * 4 + 2 * sub + 1], 64)
                for g in range(2):
                    sp.dma_start(gate[:, g, :], rows(mod_d, (l * 2 + g) * 6 * D + sub * 3 * D + 2 * D, D)).then_inc(gate_loaded, 16)

            def load_experts(l):
                def one(s, e):
                    gu, down = expert(s)
                    for w, dst, k in ((a["moe_w_gate"], gu[:, 0], KC), (a["moe_w_up"], gu[:, 1], KC), (a["moe_w_down"], down, 2)):
                        src = w[l, bass.ds(e, 1)].rearrange("o (p k) n -> p (o k) n", k=k)
                        sp.dma_start(dst, src).then_inc(expert_loaded[s], 16)
                for s in range(4):
                    one(s, s)
                if l == 0:
                    sig("psum_xs").at(sp, 2 * KC - 1)
                    load_mod(1, 0)
                with sp.Fori(1, NE // 4) as r:
                    for s in range(4):
                        sp.wait_ge(expert_free[s], r + l * (NE // 4))
                        one(s, r * 4 + s)

            def load_router(l):
                sp.dma_start(WR[:, :, 0:NG], a["moe_w_group"][l].rearrange("(p k) n -> p k n", k=KC)).then_inc(route_loaded, 16)
                sp.dma_start(WR[:, :, NG:36], a["moe_w_router"][l].rearrange("(p k) n -> p k n", k=KC)).then_inc(route_loaded, 16)
                sp.dma_start(brt[:, 0:NG], rows(a["moe_b_group"], l * NG, NG)).then_inc(route_loaded, 16)
                sp.dma_start(brt[:, NG:36], rows(a["moe_b_router"], l * NE, NE)).then_inc(route_loaded, 16)

            for k in items0[:5]:
                load(k)
            store_mod(0, 0)
            sig("cT").at(sp, 0)
            load_mod(0, 0)
            if stage >= 1:
                load(items0[5])
                load(items0[6])
                load(items0[7])
                load(items0[8])
                sp.dma_start(bias.rearrange("p a b c d -> p (a b c d)"), a["bias"]).then_inc(in_bias, 16)
                groups = {(0, 5): (0, 1), (0, 9): (0, 2), (0, 11): (0, 3), (1, 3): (1, 0), (1, 5): (1, 1), (1, 9): (1, 2), (1, 11): (1, 3)}
                for k in items0[9:]:
                    load(k)
                    n = number[k] - 2
                    if items[n][0] == "ada" and items[n][1:] in groups:
                        store_mod(*groups[items[n][1:]])
                        if items[n][1:] == (0, 5):
                            load_gate(0, 0)
            if stage >= 2:
                sig("OT").at(sp, NU // 2 - 1)
                sp.wait_ge(out_sem, 64)
                load_mod(0, 1)
                load_router(0)
                sig("xmix").at(sp, 5)
                load_experts(0)
                load_gate(0, 1)
            if stage >= 3:
                for i, k in enumerate(items1[:3]):
                    sp.wait_ge(expert_free[i], NE // 4)
                    load(k)
                sp.wait_ge(expert_free[3], NE // 4)
                for c, (nme, n) in enumerate((("hy_b_in", 24), ("hy_conv_b", 24))):
                    sp.dma_start(hrow[24 * c:24 * c + 24, :], a[nme].rearrange("o (c p) -> (o c) p", p=P)).then_inc(in_rows, 16)
                for tap in range(3):
                    sp.dma_start(hrow[48 + 24 * tap:72 + 24 * tap, :], a["hy_conv_w"][0, tap].rearrange("(c p) -> c p", p=P)).then_inc(in_rows, 16)
                for t in range(T):
                    sp.wait_ge(gathered[t], 32)
                sp.dma_start(dft, a["dft"]).then_inc(in_dft, 16)
                sig("h").at(sp, 8)
                sp.dma_start(zT[0:EMB, :], a["zt"]).then_inc(in_hy, 16)
                sp.dma_start(w1[0:EMB, :], a["hy_filt_w1"][0]).then_inc(in_hy, 16)
                sp.dma_start(w2[0:FF, :], a["hy_filt_w2"][0]).then_inc(in_hy, 16)
                for i, src in enumerate((a["hy_filt_b1"][0], a["hy_filt_freq"][0, 0], a["hy_filt_b2"][0], a["hy_filt_freq"][0, 1])):
                    sp.dma_start(fcol[0:FF, i:i + 1], src.rearrange("(p o) -> p o", o=1)).then_inc(in_hy, 16)
                sig("xffn").at(sp, 2)
                load_gate(1, 0)
                for k in items1[3:6]:
                    load(k)
                load(items1[6])

                def window(ch):
                    for t in range(T):
                        sp.dma_start(WN[:, t, :], a["win"][t * P:(t + 1) * P, ch * 512:(ch + 1) * 512]).then_inc(in_win, 16)
                    for o in range(2):
                        sp.dma_start(SK[:, o, :], rows(a["hy_skip"], o * D + ch * 512, 512)).then_inc(in_win, 16)
                sig("cv").at(sp, 23)
                sig("psum_cvT").at(sp, 15)
                window(0)
                load(items1[7])
                sig("filt").at(sp, 11)
                sig("K").at(sp, 11)
                window(1)
                load(items1[8])
            if stage >= 4:
                sig("psum_YT").at(sp, 7)
                load_mod(1, 1)
                load_router(1)
                sig("xmix").at(sp, 11)
                load_experts(1)
                load_gate(1, 1)
            else:
                for s in mod_stored:
                    sp.wait_ge(s, 64)


def bias_windows(rpb):
    half, q, t, r, c = np.ix_(range(2), range(GRID_W), range(2), range(ROWS), range(GRID_W))
    dx = np.clip(c - q + 15, 0, RPB_X - 1)
    w = rpb[0][:, 7 - 2 * t - half + r, dx]
    return np.ascontiguousarray(w.transpose(1, 2, 3, 0, 4, 5)).reshape(P, 2 * NH * ROWS * GRID_W)


INPUTS = ["x_prompt", "x_sample", "cache_mla_ckv", "cache_mla_krope", "cache_na_k", "cache_na_v", "c", "c_ctx",
          "ada_w", "ada_b", "norm_mix", "norm_ffn", "attn_w_in", "mla_q_norm", "mla_kv_norm", "mla_w_q_up",
          "mla_w_kv_up", "mla_q_gain", "mla_k_gain", "na_q_gain", "na_k_gain", "na_rpb", "attn_w_out",
          "hy_w_in", "hy_b_in", "hy_conv_w", "hy_conv_b", "hy_filt_w1", "hy_filt_b1", "hy_filt_freq", "hy_filt_w2",
          "hy_filt_b2", "hy_filt_w3", "hy_skip", "hy_w_out", "moe_w_group", "moe_b_group", "moe_w_router",
          "moe_b_router", "moe_w_gate", "moe_w_up", "moe_w_down"]
OUTPUTS = {"y_prompt": (1, SEQ, D), "y_sample": (1, DEC, D), "new_mla_ckv": (1, 1, SEQ, KVR),
           "new_mla_krope": (1, 1, SEQ, ROPE), "new_na_k": (1, 1, SEQ, NH, NAD), "new_na_v": (1, 1, SEQ, NH, NAD)}


def kernel(**inputs):
    import concourse.bacc as bacc
    from concourse.bass_utils import run_bass_kernel_spmd

    nc = bacc.Bacc("TRN2", target_bir_lowering=False, num_devices=1)
    arrays = {f"in_{n}": np.ascontiguousarray(inputs[n]) for n in INPUTS}
    zt, win = filter_positions()
    arrays["in_bias"] = bias_windows(arrays.pop("in_na_rpb"))
    arrays.update(in_tab=table(), in_dft=dft_table(), in_zt=zt, in_win=win)
    a = {k[3:]: nc.dram_tensor(k, v.shape, F32, kind="ExternalInput").ap() for k, v in arrays.items()}
    a.update({k: nc.dram_tensor(f"out_{k}", s, F32, kind="ExternalOutput").ap() for k, s in OUTPUTS.items()})
    build(nc, a)
    r = run_bass_kernel_spmd(nc, [arrays], core_ids=[0])
    return tuple(r.results[0][f"out_{k}"] for k in OUTPUTS)
```
